# Optimizing a Trainium2 kernel written in Bass

```python
import math
import jax
import jax.numpy as jnp
from jax import lax
import numpy as np
import jax, jax.numpy as jnp

D_MODEL = 1024
BATCH = 1
SEQ = 256
DEPTH = 1

GRID_W = 64
CTX_LEN = 256
NH_M = 4
DQK_M = D_MODEL // 8
DV_M = D_MODEL // 4
MLSTM_CHUNK = 128
NH_D = 8
DH_D = D_MODEL // 16
Q_BLOCK = 128
ROPE_BASE = 10000.0
N_EXPERTS = 32
TOP_K = 4
D_FF = D_MODEL
SWIGLU_LIMIT = 7.0
SWIGLU_ALPHA = 1.702
EXPERT_BLOCK = 128
NORM_EPS = 1e-6
SPLIT_SIZES = (NH_M * DQK_M, NH_M * DQK_M, NH_M * DV_M, 4 * NH_M, NH_M * DV_M,
               NH_D * 2 * DH_D, NH_D * 2 * DH_D, NH_D * 2 * DH_D, D_MODEL, D_MODEL)
IN_COLS = sum(SPLIT_SIZES)


def rmsnorm(x, g):
    xf = x.astype(jnp.float32)
    y = xf * lax.rsqrt(jnp.mean(xf * xf, axis=-1, keepdims=True) + NORM_EPS)
    return (y * g.astype(jnp.float32)).astype(x.dtype)

def modulate(u, shift, scale):
    return u * (1 + scale) + shift

def split_proj(u, w_in):
    return jnp.split(u @ w_in, np.cumsum(SPLIT_SIZES)[:-1].tolist(), axis=-1)

def axial_rope_tables(n_tok):
    rows = n_tok // GRID_W
    row = jnp.repeat(jnp.arange(rows, dtype=jnp.float32), GRID_W)
    col = jnp.tile(jnp.arange(GRID_W, dtype=jnp.float32), rows)
    n_freq = DH_D // 4
    inv_freq = ROPE_BASE ** (-jnp.arange(n_freq, dtype=jnp.float32) / n_freq)
    ang_r = (row[:, None] * inv_freq)[:, None, None, :]
    ang_c = (col[:, None] * inv_freq)[:, None, None, :]
    return (jnp.cos(ang_r), jnp.sin(ang_r), jnp.cos(ang_c), jnp.sin(ang_c))

def rotate_pairs(x, cos, sin):
    x1, x2 = jnp.split(x, 2, axis=-1)
    cos = cos.astype(x.dtype)
    sin = sin.astype(x.dtype)
    return jnp.concatenate([x1 * cos - x2 * sin, x2 * cos + x1 * sin], axis=-1)

def apply_axial_rope(x, tables):
    cos_r, sin_r, cos_c, sin_c = tables
    half = DH_D // 2
    return jnp.concatenate([rotate_pairs(x[..., :half], cos_r, sin_r),
                            rotate_pairs(x[..., half:], cos_c, sin_c)], axis=-1)

def mlstm_chunkwise(q, k, v, i_pre, logf, state):
    b_, h_, t_, _ = q.shape
    L = MLSTM_CHUNK
    nc = t_ // L

    def chunks(a):
        return jnp.moveaxis(a.reshape(a.shape[:2] + (nc, L) + a.shape[3:]), 2, 0)

    causal = jnp.tril(jnp.ones((L, L), dtype=bool))

    def step(carry, xs):
        C, n, m = carry
        qc, kc, vc, ic, fc = xs
        bcum = jnp.cumsum(fc, axis=-1)
        log_d = jnp.where(causal, bcum[..., :, None] - bcum[..., None, :] + ic[..., None, :], -jnp.inf)
        inter = bcum + m[..., None]
        m_t = jnp.maximum(inter, jnp.max(log_d, axis=-1))
        s = jnp.einsum('bhtk,bhsk->bhts', qc, kc) * jnp.exp(log_d - m_t[..., None])
        w_inter = jnp.exp(inter - m_t)
        num = w_inter[..., None] * jnp.einsum('bhtk,bhkv->bhtv', qc, C) + jnp.einsum('bhts,bhsv->bhtv', s, vc)
        den = w_inter * jnp.einsum('bhtk,bhk->bht', qc, n) + jnp.sum(s, axis=-1)
        h = num / jnp.maximum(jnp.abs(den), jnp.exp(-m_t))[..., None]
        b_last = bcum[..., -1]
        log_w = b_last[..., None] - bcum + ic
        m_new = jnp.maximum(b_last + m, jnp.max(log_w, axis=-1))
        w = jnp.exp(log_w - m_new[..., None])
        decay = jnp.exp(b_last + m - m_new)
        C_new = decay[..., None, None] * C + jnp.einsum('bhsk,bhsv->bhkv', kc * w[..., None], vc)
        n_new = decay[..., None] * n + jnp.einsum('bhs,bhsk->bhk', w, kc)
        return (C_new, n_new, m_new), h

    state, h = lax.scan(step, state, (chunks(q), chunks(k), chunks(v), chunks(i_pre), chunks(logf)))
    return jnp.moveaxis(h, 0, 2).reshape(b_, h_, t_, v.shape[-1]), state

def mlstm_zero_state(batch):
    return (jnp.zeros((batch, NH_M, DQK_M, DV_M), jnp.float32),
            jnp.zeros((batch, NH_M, DQK_M), jnp.float32),
            jnp.zeros((batch, NH_M), jnp.float32))

def mlstm_prepare(p, gate_b):
    b, t = p[0].shape[:2]

    def heads(a, d):
        return a.reshape(b, t, NH_M, d).transpose(0, 2, 1, 3).astype(jnp.float32)

    q = heads(p[0], DQK_M) * DQK_M ** -0.5
    k = heads(p[1], DQK_M)
    v = heads(p[2], DV_M)
    g = (p[3] + gate_b).astype(jnp.float32).reshape(b, t, 4, NH_M).transpose(2, 0, 3, 1)
    return q, k, v, g

def mlstm_direction(q, k, v, i_pre, f_pre, state, reverse):
    logf = jax.nn.log_sigmoid(f_pre)
    if reverse:
        q, k, v, i_pre, logf = (jnp.flip(a, axis=2) for a in (q, k, v, i_pre, logf))
    h, state = mlstm_chunkwise(q, k, v, i_pre, logf, state)
    if reverse:
        h = jnp.flip(h, axis=2)
    return h, state

def mlstm_output(h, o_raw, g):
    b, t = o_raw.shape[:2]
    hn = rmsnorm(h.transpose(0, 2, 1, 3), g)
    o = jax.nn.sigmoid(o_raw.astype(jnp.float32)).reshape(b, t, NH_M, DV_M)
    return (hn * o).reshape(b, t, NH_M * DV_M).astype(o_raw.dtype)

def diff_prepare(p, tables):
    b, t = p[5].shape[:2]
    q = p[5].reshape(b, t, NH_D, 2, DH_D)
    k = p[6].reshape(b, t, NH_D, 2, DH_D)
    if tables is not None:
        q = apply_axial_rope(q, tables)
        k = apply_axial_rope(k, tables)
    v = p[7].reshape(b, t, NH_D, 2 * DH_D)
    return q.transpose(0, 2, 3, 1, 4), k.transpose(0, 2, 3, 1, 4), v.transpose(0, 2, 1, 3)

def diff_attend(q, k, v, lam):
    s = jnp.einsum('bhmqd,bhmkd->bhmqk', q, k).astype(jnp.float32) * DH_D ** -0.5
    p = jax.nn.softmax(s, axis=-1)
    a = p[:, :, 0] - lam * p[:, :, 1]
    return jnp.einsum('bhqk,bhkd->bhqd', a.astype(v.dtype), v)

def diff_output(o, g, lam_init):
    b, h, t, d = o.shape
    on = rmsnorm(o.transpose(0, 2, 1, 3), g) * (1.0 - lam_init)
    return on.reshape(b, t, h * d)

def merge_branches(p, a_out, b_out, w_a, w_b, w_o):
    y = jax.nn.sigmoid(p[8]) * (a_out @ w_a) + jax.nn.sigmoid(p[9]) * (b_out @ w_b)
    return y @ w_o

def token_mixer(u, uc, tables, w_in, gate_b, m_norm_g, lam_p, d_norm_g, w_a, w_b, w_o, lam_init, need_ctx):
    pl = split_proj(u, w_in)
    pc = split_proj(uc, w_in)
    ql, kl, vl, gl = mlstm_prepare(pl, gate_b)
    qc, kc, vc, gc = mlstm_prepare(pc, gate_b)
    st0 = mlstm_zero_state(uc.shape[0])
    h_cf, st_f = mlstm_direction(qc, kc, vc, gc[0], gc[1], st0, False)
    h_cb, st_b = mlstm_direction(qc, kc, vc, gc[2], gc[3], st0, True)
    h_lf, _ = mlstm_direction(ql, kl, vl, gl[0], gl[1], st_f, False)
    h_lb, _ = mlstm_direction(ql, kl, vl, gl[2], gl[3], st_b, True)
    a_lat = mlstm_output(h_lf + h_lb, pl[4], m_norm_g)
    lp = lam_p.astype(jnp.float32)
    lam = jnp.exp(jnp.sum(lp[0] * lp[1])) - jnp.exp(jnp.sum(lp[2] * lp[3])) + lam_init
    qdl, kdl, vdl = diff_prepare(pl, tables)
    qdc, kdc, vdc = diff_prepare(pc, None)
    k_all = jnp.concatenate([kdc, kdl], axis=3)
    v_all = jnp.concatenate([vdc, vdl], axis=2)
    b, h, _, t, dh = qdl.shape
    n_blk = t // Q_BLOCK
    q_blocks = jnp.moveaxis(qdl.reshape(b, h, 2, n_blk, Q_BLOCK, dh), 3, 0)
    o_blocks = lax.map(lambda qb: diff_attend(qb, k_all, v_all, lam), q_blocks)
    o_lat = jnp.moveaxis(o_blocks, 0, 2).reshape(b, h, t, 2 * dh)
    b_lat = diff_output(o_lat, d_norm_g, lam_init)
    y = merge_branches(pl, a_lat, b_lat, w_a, w_b, w_o)
    if not need_ctx:
        return y, None
    a_ctx = mlstm_output(h_cf + h_cb, pc[4], m_norm_g)
    b_ctx = diff_output(diff_attend(qdc, kdc, vdc, lam), d_norm_g, lam_init)
    return y, merge_branches(pc, a_ctx, b_ctx, w_a, w_b, w_o)

def moe_ffn(u, router_w, router_b, w1, b1, w2, b2):
    b, t, d = u.shape
    n_tok = b * t
    xf = u.reshape(n_tok, d)
    logits = (xf @ router_w + router_b).astype(jnp.float32)
    top_val, top_idx = lax.top_k(logits, TOP_K)
    gate = jax.nn.softmax(top_val, axis=-1).astype(u.dtype)
    n_asg = n_tok * TOP_K
    flat_e = top_idx.reshape(n_asg)
    flat_tok = jnp.arange(n_asg, dtype=jnp.int32) // TOP_K
    order = jnp.argsort(flat_e)
    sorted_e = flat_e[order]
    counts = jnp.bincount(flat_e, length=N_EXPERTS)
    padded = (counts + EXPERT_BLOCK - 1) // EXPERT_BLOCK * EXPERT_BLOCK
    pad_end = jnp.cumsum(padded)
    pad_start = pad_end - padded
    sorted_start = jnp.cumsum(counts) - counts
    dest = pad_start[sorted_e] + jnp.arange(n_asg) - sorted_start[sorted_e]
    n_buf = -(-n_asg // EXPERT_BLOCK) * EXPERT_BLOCK + N_EXPERTS * EXPERT_BLOCK
    buf_tok = jnp.zeros((n_buf,), jnp.int32).at[dest].set(flat_tok[order])
    buf_w = jnp.zeros((n_buf,), u.dtype).at[dest].set(gate.reshape(n_asg)[order])
    n_blk = n_buf // EXPERT_BLOCK
    blk_e = jnp.minimum(jnp.searchsorted(pad_end, jnp.arange(n_blk) * EXPERT_BLOCK, side='right'), N_EXPERTS - 1)

    def expert_block(args):
        tok, e = args
        hcat = xf[tok] @ w1[e] + b1[e]
        h_glu = jnp.minimum(hcat[:, :D_FF], SWIGLU_LIMIT)
        h_lin = jnp.clip(hcat[:, D_FF:], -SWIGLU_LIMIT, SWIGLU_LIMIT)
        act = h_glu * jax.nn.sigmoid(SWIGLU_ALPHA * h_glu) * (h_lin + 1)
        return act @ w2[e] + b2[e]

    y_buf = lax.map(expert_block, (buf_tok.reshape(n_blk, EXPERT_BLOCK), blk_e))
    y = jax.ops.segment_sum(y_buf.reshape(n_buf, d) * buf_w[:, None], buf_tok, num_segments=n_tok)
    return y.reshape(b, t, d)

def first_inputs(seed: int = 0) -> dict:
    key = jax.random.key(seed)
    ks = jax.random.split(key, 24)

    def nrm(k, shape, scale):
        return jax.random.normal(k, shape, jnp.float32) * scale

    L = DEPTH
    gate_base = jnp.array([0.0, 3.0, 0.0, 3.0], jnp.float32)[None, :, None]
    return {
        'x': nrm(ks[0], (BATCH, SEQ, D_MODEL), 1.0),
        'c': nrm(ks[1], (BATCH, D_MODEL), 1.0),
        'ctx': nrm(ks[2], (BATCH, CTX_LEN, D_MODEL), 1.0),
        'c_ctx': nrm(ks[3], (D_MODEL,), 1.0),
        'ada_w': nrm(ks[4], (L, D_MODEL, 6 * D_MODEL), 0.5 * D_MODEL ** -0.5),
        'ada_b': nrm(ks[5], (L, 6 * D_MODEL), 0.02),
        'norm1_g': 1.0 + nrm(ks[6], (L, D_MODEL), 0.02),
        'norm2_g': 1.0 + nrm(ks[7], (L, D_MODEL), 0.02),
        'w_in': nrm(ks[8], (L, D_MODEL, IN_COLS), D_MODEL ** -0.5),
        'mlstm_gate_b': (gate_base + nrm(ks[9], (L, 4, NH_M), 0.1)).reshape(L, 4 * NH_M),
        'mlstm_norm_g': 1.0 + nrm(ks[10], (L, NH_M, DV_M), 0.02),
        'diff_lambda': nrm(ks[11], (L, 4, DH_D), 0.1),
        'diff_norm_g': 1.0 + nrm(ks[12], (L, NH_D, 2 * DH_D), 0.02),
        'w_branch_a': nrm(ks[13], (L, NH_M * DV_M, D_MODEL), (NH_M * DV_M) ** -0.5),
        'w_branch_b': nrm(ks[14], (L, NH_D * 2 * DH_D, D_MODEL), (NH_D * 2 * DH_D) ** -0.5),
        'w_out': nrm(ks[15], (L, D_MODEL, D_MODEL), D_MODEL ** -0.5),
        'router_w': nrm(ks[16], (L, D_MODEL, N_EXPERTS), D_MODEL ** -0.5),
        'router_b': nrm(ks[17], (L, N_EXPERTS), 0.01),
        'exp_w1': nrm(ks[18], (L, N_EXPERTS, D_MODEL, 2 * D_FF), D_MODEL ** -0.5),
        'exp_b1': nrm(ks[19], (L, N_EXPERTS, 2 * D_FF), 0.01),
        'exp_w2': nrm(ks[20], (L, N_EXPERTS, D_FF, D_MODEL), D_FF ** -0.5),
        'exp_b2': nrm(ks[21], (L, N_EXPERTS, D_MODEL), 0.01),
        'final_norm_g': 1.0 + nrm(ks[22], (D_MODEL,), 0.02),
    }

def first_block(x, c, ctx, c_ctx, ada_w, ada_b, norm1_g, norm2_g, w_in, mlstm_gate_b, mlstm_norm_g,
              diff_lambda, diff_norm_g, w_branch_a, w_branch_b, w_out, router_w, router_b,
              exp_w1, exp_b1, exp_w2, exp_b2, final_norm_g):
    tables = axial_rope_tables(x.shape[1])
    xc = ctx
    for l in range(DEPTH):
        need_ctx = l < DEPTH - 1
        lam_init = 0.8 - 0.6 * math.exp(-0.3 * l)
        mod = jax.nn.silu(c) @ ada_w[l] + ada_b[l]
        sh1, sc1, g1, sh2, sc2, g2 = jnp.split(mod[:, None, :], 6, axis=-1)
        modc = jax.nn.silu(c_ctx) @ ada_w[l] + ada_b[l]
        sh1c, sc1c, g1c, sh2c, sc2c, g2c = jnp.split(modc, 6, axis=-1)
        u = modulate(rmsnorm(x, norm1_g[l]), sh1, sc1)
        uc = modulate(rmsnorm(xc, norm1_g[l]), sh1c, sc1c)
        y, yc = token_mixer(u, uc, tables, w_in[l], mlstm_gate_b[l], mlstm_norm_g[l], diff_lambda[l],
                            diff_norm_g[l], w_branch_a[l], w_branch_b[l], w_out[l], lam_init, need_ctx)
        x = x + g1 * y
        x = x + g2 * moe_ffn(modulate(rmsnorm(x, norm2_g[l]), sh2, sc2), router_w[l], router_b[l],
                             exp_w1[l], exp_b1[l], exp_w2[l], exp_b2[l])
        if need_ctx:
            xc = xc + g1c * yc
            xc = xc + g2c * moe_ffn(modulate(rmsnorm(xc, norm2_g[l]), sh2c, sc2c), router_w[l], router_b[l],
                                    exp_w1[l], exp_b1[l], exp_w2[l], exp_b2[l])
    return rmsnorm(x, final_norm_g)


DEPTH_2 = 2

N_META = 16
BLOCK = 128
PAD = BLOCK - N_META

D_RNN = D_MODEL
LRU_BLOCKS = 8
LRU_BS = D_RNN // LRU_BLOCKS
LRU_C = 8.0
CONV_A = 4

N_Q_HEADS = 16
N_KV_HEADS = 2
HEAD_DIM = 64
Q_PER_KV = N_Q_HEADS // N_KV_HEADS
WINDOW = 128
Q_DIM = N_Q_HEADS * HEAD_DIM
KV_DIM = N_KV_HEADS * HEAD_DIM

EVEN_IN = 2 * D_RNN + Q_DIM + 2 * KV_DIM
EVEN_MIX = D_RNN + Q_DIM

D_SSM = 2 * D_MODEL
SSD_HEADDIM = 64
SSD_HEADS = D_SSM // SSD_HEADDIM
SSD_GROUPS = 8
SSD_HPG = SSD_HEADS // SSD_GROUPS
SSD_STATE = 128
CONV_C = 4
SSD_CONV_DIM = D_SSM + 2 * SSD_GROUPS * SSD_STATE
ODD_IN = D_SSM + SSD_CONV_DIM + SSD_HEADS

D_FF_2 = 2816
CONV_F = 3

EPS = 1e-6


def rms_norm(x, w):
    x32 = x.astype(jnp.float32)
    y = x32 * lax.rsqrt(jnp.mean(x32 * x32, axis=-1, keepdims=True) + EPS)
    return (y * w.astype(jnp.float32)).astype(x.dtype)

def causal_dwconv(x, w, b):
    k = w.shape[0]
    y = lax.conv_general_dilated(
        x, w[:, None, :].astype(x.dtype), window_strides=(1,), padding=[(k - 1, 0)],
        dimension_numbers=("NWC", "WIO", "NWC"), feature_group_count=x.shape[-1])
    return y + b.astype(x.dtype)

def alibi_slopes(n_heads):
    return 2.0 ** (-8.0 * jnp.arange(1, n_heads + 1, dtype=jnp.float32) / n_heads)

def rg_lru(x, w_a, b_a, w_x, b_x, lam):
    bsz, L, _ = x.shape
    x32 = x.astype(jnp.float32)
    xb = x32.reshape(bsz, L, LRU_BLOCKS, LRU_BS)
    r = jax.nn.sigmoid(jnp.einsum("blni,nij->blnj", xb, w_a.astype(jnp.float32)).reshape(bsz, L, D_RNN) + b_a)
    i = jax.nn.sigmoid(jnp.einsum("blni,nij->blnj", xb, w_x.astype(jnp.float32)).reshape(bsz, L, D_RNN) + b_x)
    log_a = -LRU_C * r * jax.nn.softplus(-lam.astype(jnp.float32))
    a = jnp.exp(log_a)
    u = jnp.sqrt(-jnp.expm1(2.0 * log_a)) * (i * x32)

    def combine(c1, c2):
        a1, b1 = c1
        a2, b2 = c2
        return a1 * a2, a2 * b1 + b2

    _, h = lax.associative_scan(combine, (a, u), axis=1)
    return h.astype(x.dtype)

def swa_sink_alibi(q, k, v, sinks):
    bsz, L = q.shape[:2]
    Lp = L + PAD
    nblk = Lp // BLOCK
    q = q.astype(jnp.float32)
    k = k.astype(jnp.float32)
    v = v.astype(jnp.float32)
    padw = ((0, 0), (PAD, 0), (0, 0), (0, 0))
    qb = jnp.pad(q, padw).reshape(bsz, nblk, BLOCK, N_KV_HEADS, Q_PER_KV, HEAD_DIM)
    kb = jnp.pad(k, padw).reshape(bsz, nblk, BLOCK, N_KV_HEADS, HEAD_DIM)
    vb = jnp.pad(v, padw).reshape(bsz, nblk, BLOCK, N_KV_HEADS, HEAD_DIM)
    shift = ((0, 0), (1, 0), (0, 0), (0, 0), (0, 0))
    k_band = jnp.concatenate([jnp.pad(kb, shift)[:, :-1], kb], axis=2)
    v_band = jnp.concatenate([jnp.pad(vb, shift)[:, :-1], vb], axis=2)
    k_meta = k[:, :N_META]
    v_meta = v[:, :N_META]
    scale = HEAD_DIM ** -0.5
    s_band = jnp.einsum("bnqkgd,bnskd->bnkgqs", qb, k_band) * scale
    s_meta = jnp.einsum("bnqkgd,bmkd->bnkgqm", qb, k_meta) * scale

    blk = jnp.arange(nblk)
    t = blk[:, None] * BLOCK + jnp.arange(BLOCK)[None, :] - PAD
    s = (blk[:, None] - 1) * BLOCK + jnp.arange(2 * BLOCK)[None, :] - PAD
    dist_band = t[:, :, None] - s[:, None, :]
    band_ok = (s[:, None, :] >= N_META) & (dist_band >= 0) & (dist_band < WINDOW)
    dist_meta = t[:, :, None] - jnp.arange(N_META)[None, None, :]
    meta_ok = dist_meta >= 0

    slopes = alibi_slopes(N_Q_HEADS).reshape(N_KV_HEADS, Q_PER_KV)[:, :, None, None]
    pen_band = slopes * dist_band[:, None, None].astype(jnp.float32)
    pen_meta = slopes * jnp.minimum(dist_meta, WINDOW)[:, None, None].astype(jnp.float32)
    s_band = jnp.where(band_ok[:, None, None], s_band - pen_band, -jnp.inf)
    s_meta = jnp.where(meta_ok[:, None, None], s_meta - pen_meta, -jnp.inf)

    sink = sinks.astype(jnp.float32).reshape(N_KV_HEADS, Q_PER_KV)[:, :, None, None]
    mx = jnp.maximum(jnp.maximum(s_band.max(-1, keepdims=True), s_meta.max(-1, keepdims=True)), sink)
    p_band = jnp.exp(s_band - mx)
    p_meta = jnp.exp(s_meta - mx)
    denom = p_band.sum(-1, keepdims=True) + p_meta.sum(-1, keepdims=True) + jnp.exp(sink - mx)
    p_band = p_band / denom
    p_meta = p_meta / denom
    o = (jnp.einsum("bnkgqs,bnskd->bnqkgd", p_band, v_band)
         + jnp.einsum("bnkgqm,bmkd->bnqkgd", p_meta, v_meta))
    return o.reshape(bsz, Lp, Q_DIM)[:, PAD:]

def griffin_swa_mixer(u, w_in, conv_w, conv_b, w_a, b_a, w_x, b_x, lam, sinks, w_out):
    bsz, L, _ = u.shape
    proj = u @ w_in
    gate, xr, q, k, v = jnp.split(
        proj, [D_RNN, 2 * D_RNN, 2 * D_RNN + Q_DIM, 2 * D_RNN + Q_DIM + KV_DIM], axis=-1)
    xr = causal_dwconv(xr, conv_w, conv_b)
    y_a = jax.nn.gelu(gate, approximate=True) * rg_lru(xr, w_a, b_a, w_x, b_x, lam)
    y_b = swa_sink_alibi(q.reshape(bsz, L, N_Q_HEADS, HEAD_DIM),
                         k.reshape(bsz, L, N_KV_HEADS, HEAD_DIM),
                         v.reshape(bsz, L, N_KV_HEADS, HEAD_DIM), sinks).astype(u.dtype)
    return jnp.concatenate([y_a, y_b], axis=-1) @ w_out

def ssd_chunked(x, dt, a, b_in, c_in):
    bsz, Lp = x.shape[:2]
    nc = Lp // BLOCK
    x = x.reshape(bsz, nc, BLOCK, SSD_GROUPS, SSD_HPG, SSD_HEADDIM)
    dt = dt.reshape(bsz, nc, BLOCK, SSD_GROUPS, SSD_HPG)
    bc = b_in.reshape(bsz, nc, BLOCK, SSD_GROUPS, SSD_STATE)
    cc = c_in.reshape(bsz, nc, BLOCK, SSD_GROUPS, SSD_STATE)
    cs = jnp.cumsum(dt * a.reshape(SSD_GROUPS, SSD_HPG), axis=2)
    xdt = x * dt[..., None]
    cs_t = jnp.moveaxis(cs, 2, -1)
    seg = cs_t[..., :, None] - cs_t[..., None, :]
    tril = jnp.tril(jnp.ones((BLOCK, BLOCK), dtype=bool))
    decay_in = jnp.exp(jnp.where(tril, seg, -jnp.inf))
    cb = jnp.einsum("bclgn,bcsgn->bcgls", cc, bc)
    y_diag = jnp.einsum("bcgls,bcghls,bcsghp->bclghp", cb, decay_in, xdt)
    cs_last = cs[:, :, -1:]
    chunk_states = jnp.einsum("bclgn,bclgh,bclghp->bcghpn", bc, jnp.exp(cs_last - cs), xdt)
    chunk_decay = jnp.exp(cs_last[:, :, 0])

    def step(state, inp):
        dec, st = inp
        return state * dec[..., None, None] + st, state

    init = jnp.zeros_like(chunk_states[:, 0])
    _, prev = lax.scan(step, init, (jnp.moveaxis(chunk_decay, 1, 0), jnp.moveaxis(chunk_states, 1, 0)))
    prev = jnp.moveaxis(prev, 0, 1)
    y_off = jnp.einsum("bclgn,bcghpn,bclgh->bclghp", cc, prev, jnp.exp(cs))
    return (y_diag + y_off).reshape(bsz, Lp, SSD_HEADS, SSD_HEADDIM)

def mamba2_mixer(u, w_in, conv_w, conv_b, dt_bias, a_log, d_skip, gate_norm, w_out):
    bsz, L, _ = u.shape
    proj = u @ w_in
    z, xbc, dt = jnp.split(proj, [D_SSM, D_SSM + SSD_CONV_DIM], axis=-1)
    xbc = jax.nn.silu(causal_dwconv(xbc, conv_w, conv_b))
    xs, bs, cs = jnp.split(xbc, [D_SSM, D_SSM + SSD_GROUPS * SSD_STATE], axis=-1)
    xs = xs.reshape(bsz, L, SSD_HEADS, SSD_HEADDIM).astype(jnp.float32)
    bs = bs.reshape(bsz, L, SSD_GROUPS, SSD_STATE).astype(jnp.float32)
    cs = cs.reshape(bsz, L, SSD_GROUPS, SSD_STATE).astype(jnp.float32)
    dt = jax.nn.softplus(dt.astype(jnp.float32) + dt_bias.astype(jnp.float32))
    a = -jnp.exp(a_log.astype(jnp.float32))

    def front_pad(t):
        return jnp.pad(t, ((0, 0), (PAD, 0)) + ((0, 0),) * (t.ndim - 2))

    y = ssd_chunked(front_pad(xs), front_pad(dt), a, front_pad(bs), front_pad(cs))[:, PAD:]
    y = y + d_skip.astype(jnp.float32)[:, None] * xs
    y = y.reshape(bsz, L, D_SSM) * jax.nn.silu(z.astype(jnp.float32))
    yg = y.reshape(bsz, L, SSD_GROUPS, D_SSM // SSD_GROUPS)
    yg = yg * lax.rsqrt(jnp.mean(yg * yg, axis=-1, keepdims=True) + EPS)
    y = yg.reshape(bsz, L, D_SSM) * gate_norm.astype(jnp.float32)
    return y.astype(u.dtype) @ w_out

def conv_ffn(u, w_up, conv_w, conv_b, w_down):
    h = causal_dwconv(u @ w_up, conv_w, conv_b)
    g, up = jnp.split(h, 2, axis=-1)
    return (jax.nn.gelu(g, approximate=True) * up) @ w_down

def second_inputs(seed: int = 0) -> dict:
    key = jax.random.key(seed)
    k = jax.random.split(key, 36)

    def normal(kk, shape, scale):
        return jax.random.normal(kk, shape, jnp.float32) * scale

    def gain(kk, n):
        return 1.0 + 0.05 * jax.random.normal(kk, (n,), jnp.float32)

    u = jax.random.uniform(k[11], (D_RNN,), jnp.float32, 0.9, 0.999)
    a0 = u ** (1.0 / LRU_C)
    lru_lambda = jnp.log(a0) - jnp.log1p(-a0)
    dt0 = jnp.exp(jax.random.uniform(k[25], (SSD_HEADS,), jnp.float32, math.log(1e-3), math.log(1e-1)))
    dt_bias = dt0 + jnp.log(-jnp.expm1(-dt0))
    a_log = jnp.log(jax.random.uniform(k[26], (SSD_HEADS,), jnp.float32, 1.0, 16.0))

    return {
        "x": normal(k[0], (BATCH, SEQ, D_MODEL), 1.0),
        "meta_tokens": normal(k[1], (N_META, D_MODEL), 1.0),
        "l0_mix_pre_norm": gain(k[2], D_MODEL),
        "l0_mix_post_norm": gain(k[3], D_MODEL),
        "l0_w_in": normal(k[4], (D_MODEL, EVEN_IN), D_MODEL ** -0.5),
        "l0_lru_conv_w": normal(k[5], (CONV_A, D_RNN), CONV_A ** -0.5),
        "l0_lru_conv_b": normal(k[6], (D_RNN,), 0.01),
        "l0_lru_w_a": normal(k[7], (LRU_BLOCKS, LRU_BS, LRU_BS), LRU_BS ** -0.5),
        "l0_lru_b_a": normal(k[8], (D_RNN,), 0.01),
        "l0_lru_w_x": normal(k[9], (LRU_BLOCKS, LRU_BS, LRU_BS), LRU_BS ** -0.5),
        "l0_lru_b_x": normal(k[10], (D_RNN,), 0.01),
        "l0_lru_lambda": lru_lambda,
        "l0_attn_sinks": normal(k[12], (N_Q_HEADS,), 0.5),
        "l0_w_out": normal(k[13], (EVEN_MIX, D_MODEL), EVEN_MIX ** -0.5),
        "l0_ffn_pre_norm": gain(k[14], D_MODEL),
        "l0_ffn_post_norm": gain(k[15], D_MODEL),
        "l0_ffn_w_up": normal(k[16], (D_MODEL, 2 * D_FF_2), D_MODEL ** -0.5),
        "l0_ffn_conv_w": normal(k[17], (CONV_F, 2 * D_FF_2), CONV_F ** -0.5),
        "l0_ffn_conv_b": normal(k[18], (2 * D_FF_2,), 0.01),
        "l0_ffn_w_down": normal(k[19], (D_FF_2, D_MODEL), D_FF_2 ** -0.5),
        "l1_mix_pre_norm": gain(k[20], D_MODEL),
        "l1_mix_post_norm": gain(k[21], D_MODEL),
        "l1_w_in": normal(k[22], (D_MODEL, ODD_IN), D_MODEL ** -0.5),
        "l1_ssm_conv_w": normal(k[23], (CONV_C, SSD_CONV_DIM), CONV_C ** -0.5),
        "l1_ssm_conv_b": normal(k[24], (SSD_CONV_DIM,), 0.01),
        "l1_dt_bias": dt_bias,
        "l1_a_log": a_log,
        "l1_d_skip": 1.0 + 0.1 * jax.random.normal(k[27], (SSD_HEADS,), jnp.float32),
        "l1_gate_norm": gain(k[28], D_SSM),
        "l1_w_out": normal(k[29], (D_SSM, D_MODEL), D_SSM ** -0.5),
        "l1_ffn_pre_norm": gain(k[30], D_MODEL),
        "l1_ffn_post_norm": gain(k[31], D_MODEL),
        "l1_ffn_w_up": normal(k[32], (D_MODEL, 2 * D_FF_2), D_MODEL ** -0.5),
        "l1_ffn_conv_w": normal(k[33], (CONV_F, 2 * D_FF_2), CONV_F ** -0.5),
        "l1_ffn_conv_b": normal(k[34], (2 * D_FF_2,), 0.01),
        "l1_ffn_w_down": normal(k[35], (D_FF_2, D_MODEL), D_FF_2 ** -0.5),
    }

def second_block(x, meta_tokens,
              l0_mix_pre_norm, l0_mix_post_norm, l0_w_in, l0_lru_conv_w, l0_lru_conv_b,
              l0_lru_w_a, l0_lru_b_a, l0_lru_w_x, l0_lru_b_x, l0_lru_lambda, l0_attn_sinks, l0_w_out,
              l0_ffn_pre_norm, l0_ffn_post_norm, l0_ffn_w_up, l0_ffn_conv_w, l0_ffn_conv_b, l0_ffn_w_down,
              l1_mix_pre_norm, l1_mix_post_norm, l1_w_in, l1_ssm_conv_w, l1_ssm_conv_b,
              l1_dt_bias, l1_a_log, l1_d_skip, l1_gate_norm, l1_w_out,
              l1_ffn_pre_norm, l1_ffn_post_norm, l1_ffn_w_up, l1_ffn_conv_w, l1_ffn_conv_b, l1_ffn_w_down):
    bsz = x.shape[0]
    meta = jnp.broadcast_to(meta_tokens.astype(x.dtype)[None], (bsz, N_META, D_MODEL))
    h = jnp.concatenate([meta, x], axis=1)
    layers = [
        (l0_mix_pre_norm, l0_mix_post_norm,
         (l0_w_in, l0_lru_conv_w, l0_lru_conv_b, l0_lru_w_a, l0_lru_b_a, l0_lru_w_x, l0_lru_b_x,
          l0_lru_lambda, l0_attn_sinks, l0_w_out),
         (l0_ffn_pre_norm, l0_ffn_post_norm, l0_ffn_w_up, l0_ffn_conv_w, l0_ffn_conv_b, l0_ffn_w_down)),
        (l1_mix_pre_norm, l1_mix_post_norm,
         (l1_w_in, l1_ssm_conv_w, l1_ssm_conv_b, l1_dt_bias, l1_a_log, l1_d_skip, l1_gate_norm, l1_w_out),
         (l1_ffn_pre_norm, l1_ffn_post_norm, l1_ffn_w_up, l1_ffn_conv_w, l1_ffn_conv_b, l1_ffn_w_down)),
    ]
    for i in range(DEPTH_2):
        pre, post, mix, ffn = layers[i]
        mixer = griffin_swa_mixer if i % 2 == 0 else mamba2_mixer
        h = h + rms_norm(mixer(rms_norm(h, pre), *mix), post)
        f_pre, f_post, w_up, c_w, c_b, w_down = ffn
        h = h + rms_norm(conv_ffn(rms_norm(h, f_pre), w_up, c_w, c_b, w_down), f_post)
    return h[:, N_META:]


def setup_inputs(seed=0):
    out = dict(first_inputs(seed))
    for name, value in second_inputs(seed + 1).items():
        if name != "x":
            out[name + "_2"] = value
    return out


def reference(
    x, c, ctx, c_ctx, ada_w, ada_b, norm1_g, norm2_g, w_in, mlstm_gate_b, mlstm_norm_g,
    diff_lambda, diff_norm_g, w_branch_a, w_branch_b, w_out, router_w, router_b, exp_w1, exp_b1,
    exp_w2, exp_b2, final_norm_g, meta_tokens_2, l0_mix_pre_norm_2, l0_mix_post_norm_2,
    l0_w_in_2, l0_lru_conv_w_2, l0_lru_conv_b_2, l0_lru_w_a_2, l0_lru_b_a_2, l0_lru_w_x_2,
    l0_lru_b_x_2, l0_lru_lambda_2, l0_attn_sinks_2, l0_w_out_2, l0_ffn_pre_norm_2,
    l0_ffn_post_norm_2, l0_ffn_w_up_2, l0_ffn_conv_w_2, l0_ffn_conv_b_2, l0_ffn_w_down_2,
    l1_mix_pre_norm_2, l1_mix_post_norm_2, l1_w_in_2, l1_ssm_conv_w_2, l1_ssm_conv_b_2,
    l1_dt_bias_2, l1_a_log_2, l1_d_skip_2, l1_gate_norm_2, l1_w_out_2, l1_ffn_pre_norm_2,
    l1_ffn_post_norm_2, l1_ffn_w_up_2, l1_ffn_conv_w_2, l1_ffn_conv_b_2, l1_ffn_w_down_2,
):
    x = first_block(
        x, c, ctx, c_ctx, ada_w, ada_b, norm1_g, norm2_g, w_in, mlstm_gate_b, mlstm_norm_g,
        diff_lambda, diff_norm_g, w_branch_a, w_branch_b, w_out, router_w, router_b, exp_w1,
        exp_b1, exp_w2, exp_b2, final_norm_g,
    )
    return second_block(
        x, meta_tokens_2, l0_mix_pre_norm_2, l0_mix_post_norm_2, l0_w_in_2, l0_lru_conv_w_2,
        l0_lru_conv_b_2, l0_lru_w_a_2, l0_lru_b_a_2, l0_lru_w_x_2, l0_lru_b_x_2,
        l0_lru_lambda_2, l0_attn_sinks_2, l0_w_out_2, l0_ffn_pre_norm_2, l0_ffn_post_norm_2,
        l0_ffn_w_up_2, l0_ffn_conv_w_2, l0_ffn_conv_b_2, l0_ffn_w_down_2, l1_mix_pre_norm_2,
        l1_mix_post_norm_2, l1_w_in_2, l1_ssm_conv_w_2, l1_ssm_conv_b_2, l1_dt_bias_2,
        l1_a_log_2, l1_d_skip_2, l1_gate_norm_2, l1_w_out_2, l1_ffn_pre_norm_2,
        l1_ffn_post_norm_2, l1_ffn_w_up_2, l1_ffn_conv_w_2, l1_ffn_conv_b_2, l1_ffn_w_down_2,
    )


_drawn_inputs = setup_inputs


def setup_inputs(seed=0):
    import zlib

    import numpy as np

    out = dict(_drawn_inputs(seed))
    spreads = {}
    factors = {'mlstm_norm_g': 15.088,
     'diff_norm_g': 9.536,
     'router_b': 3.156,
     'exp_b1': 8.0,
     'exp_b2': 37.553,
     'l0_lru_b_a_2': 40.372,
     'l0_lru_b_x_2': 8.0,
     'l0_ffn_conv_b_2': 5.439,
     'l1_ssm_conv_b_2': 7.747,
     'l1_ffn_conv_b_2': 8.0,
     'norm2_g': 2.673}
    for name, (base, spread) in spreads.items():
        noise = np.random.default_rng([zlib.crc32(name.encode()), seed]).standard_normal(out[name].shape)
        drawn = base * np.exp(spread * noise) if base else spread * noise
        out[name] = jnp.asarray(drawn.astype(out[name].dtype))
    for name, factor in factors.items():
        out[name] = (out[name] * factor).astype(out[name].dtype)
    return out
```

```python
import math
from contextlib import ExitStack

import concourse.bass as bass
from concourse import mybir
import numpy as np

F32 = mybir.dt.float32
I32 = mybir.dt.int32
U32 = mybir.dt.uint32
ALU = mybir.AluOpType
ACT = mybir.ActivationFunctionType
AX_X = mybir.AxisListType.X

P = 128
D = 1024
KT = D // P
T = 256
TT = T // P
EPS = 1e-6

NH_M, DV_M = 4, 256
NH_D, DH_D = 8, 64
LAM_INIT = 0.8 - 0.6 * math.exp(-0.3 * 0)
GRID_W, ROPE_BASE = 64, 10000.0

NE, TOPK, FF = 32, 4, 1024
SLOTS = 96
PASSES = -(-T // SLOTS)
LIMIT, ALPHA = 7.0, 1.702
GROUP = 32
ROUNDS = [[(0, 0), (0, 1), (0, 2), (1, 0)], [(2, 0), (2, 1), (1, 1), (1, 2)], [(3, 0), (3, 1), (3, 2), (2, 2)]]

GATE_BANKS, LINEAR_BANKS = (3, 0, 1), (4, 5, 2)

ROW_BANKS = (2, 3, 6)


def pieces(tasks):
    out = []
    for j, (b, g) in enumerate(tasks):
        if out and out[-1][1] == b and out[-1][2] + out[-1][3] == g:
            q, b0, g0, n = out.pop()
            out.append((q, b0, g0, n + 1))
        else:
            out.append((j, b, g, 1))
    return out

META = 16
L = META + T
HEADS2, HD = 16, 64
SLOPES = [2.0 ** (-8.0 * (i + 1) / HEADS2) for i in range(HEADS2)]
FF2 = 2816
FT = FF2 // P
DS = 2 * D
ST = DS // P
SH, SG = 32, 8
CT = 32
LRU_C = 8.0
TOK = [(0, 128), (128, 128), (256, 16)]
SEG = [0, 272, 416]
STRIP = 432

R = 6
UW = 2048
NL = 2


def layout(items):
    at, out = 0, {}
    for name, n in items:
        out[name] = (at, n)
        at += n
    return out, at


PARAM, NPARAM = layout([
    ("c", 2 * KT), ("ada_b", 48), ("norm1_g", 8), ("norm2_g", 8), ("final_g", 8), ("mnorm_g", 8),
    ("dnorm_g", 8), ("lam_p", 4), ("gate_b", 16), ("router_b", NE), ("b1", NE * 16),
    ("l0_pre", 8), ("l0_post", 8), ("lru_cw", 32), ("lru_cb", 8), ("lru_ba", 8), ("lru_bx", 8),
    ("lru_lam", 8), ("sinks", HEADS2), ("f0_pre", 8), ("f0_post", 8), ("f0_cw", 3 * 44), ("f0_cb", 44),
    ("l1_pre", 8), ("l1_post", 8), ("ssm_cw", 4 * CT), ("ssm_cb", CT), ("dt_bias", 1), ("a_log", 1),
    ("d_skip", ST), ("gnorm", ST), ("f1_pre", 8), ("f1_post", 8), ("f1_cw", 3 * 44), ("f1_cb", 44)])

CONST, NCONST = layout([
    ("ident", P), ("ones", P), ("before", P), ("perm", P), ("mask", 2 * 512), ("cos", T), ("sin", T),
    ("slot", SLOTS), ("iota", NE), ("slope", HEADS2), ("pen", 3 * P + L), ("causal", STRIP), ("eps", 1)])
PEN_OFF = -1.0e30


def constants():
    out = np.zeros((P, NCONST), np.float32)

    def put(name, value):
        at, n = CONST[name]
        out[:, at:at + n] = np.asarray(value, np.float32).reshape(-1, n)

    p, j = np.arange(P)[:, None], np.arange(P)[None, :]
    put("ident", p == j)
    put("ones", np.ones((P, P)))
    put("before", p < j)
    perm = np.zeros((P, P), np.float32)
    for m in range(P):
        if m % 32 < 16:
            perm[m + 16, m] = -1.0
        else:
            perm[m - 16, m] = 1.0
    put("perm", perm)
    t = np.arange(T)[None, :]
    put("mask", np.concatenate([p <= t, p + P <= t, p >= t, p + P >= t], axis=1))
    row, col = t[0] // GRID_W, t[0] % GRID_W
    nf = DH_D // 4
    freq = ROPE_BASE ** (-np.arange(nf) / nf)
    ang = np.zeros((P, T))
    for m in range(P):
        ang[m] = (row if m % 64 < 32 else col) * freq[m % 16]
    put("cos", np.cos(ang))
    put("sin", np.sin(ang))
    put("slot", np.arange(SLOTS)[None, :] + 0.0)
    put("iota", np.arange(NE)[None, :] + 0.0)
    put("slope", np.array([SLOPES[j + 8 * s] for j in range(8) for s in range(2)])[None, :] * HD ** 0.5)
    pen = np.full((P, 3, L), PEN_OFF)
    for i, (t0, n) in enumerate(TOK):
        q = np.arange(t0, t0 + n)[:, None]
        s = np.arange(L)[None, :]
        dist = q - s
        band = (s >= META) & (dist >= 0) & (dist < P)
        meta = (s < META) & (dist >= 0)
        pen[:n, i] = np.where(band, -dist, np.where(meta, -np.minimum(dist, P), PEN_OFF))
    put("pen", np.concatenate([pen[:, i, :t0 + n] for i, (t0, n) in enumerate(TOK)], axis=1))
    strip = np.zeros((P, STRIP))
    for i, (t0, n) in enumerate(TOK):
        strip[:, SEG[i]:SEG[i] + L - t0] = (p + t0) <= np.arange(t0, L)[None, :]
    put("causal", strip)
    put("eps", np.full((P, 1), EPS))
    return out


def columns(a):
    a = np.asarray(a, np.float32).reshape(-1, P)
    return a.T


def pack_params(i):
    out = np.zeros((P, NPARAM), np.float32)

    def put(name, value):
        at, n = PARAM[name]
        out[:, at:at + n] = np.asarray(value).reshape(-1, n)

    both = np.stack([i["c"][0], i["c_ctx"]])
    put("c", both.reshape(2, KT, P).transpose(2, 1, 0))
    put("ada_b", columns(i["ada_b"]))
    put("norm1_g", columns(i["norm1_g"]))
    put("norm2_g", columns(i["norm2_g"]))
    put("final_g", columns(i["final_norm_g"]))
    put("mnorm_g", columns(i["mlstm_norm_g"]))
    put("dnorm_g", columns(i["diff_norm_g"]))
    lam = np.zeros((P, 4), np.float32)
    lam[:DH_D] = i["diff_lambda"][0].T
    put("lam_p", lam)
    put("gate_b", i["mlstm_gate_b"])
    put("router_b", i["router_b"])
    put("b1", columns(i["exp_b1"]).reshape(P, NE, 2, 4, 2).transpose(0, 1, 3, 2, 4))
    put("l0_pre", columns(i["l0_mix_pre_norm_2"]))
    put("l0_post", columns(i["l0_mix_post_norm_2"]))
    put("lru_cw", columns(i["l0_lru_conv_w_2"]))
    put("lru_cb", columns(i["l0_lru_conv_b_2"]))
    put("lru_ba", columns(i["l0_lru_b_a_2"]))
    put("lru_bx", columns(i["l0_lru_b_x_2"]))
    put("lru_lam", columns(i["l0_lru_lambda_2"]))
    put("sinks", i["l0_attn_sinks_2"].reshape(2, 8).T)
    for n in (0, 1):
        put(f"f{n}_pre", columns(i[f"l{n}_ffn_pre_norm_2"]))
        put(f"f{n}_post", columns(i[f"l{n}_ffn_post_norm_2"]))
        put(f"f{n}_cw", columns(i[f"l{n}_ffn_conv_w_2"]).reshape(P, 3, 2, FT).transpose(0, 1, 3, 2))
        put(f"f{n}_cb", columns(i[f"l{n}_ffn_conv_b_2"]).reshape(P, 2, FT).transpose(0, 2, 1))
    put("l1_pre", columns(i["l1_mix_pre_norm_2"]))
    put("l1_post", columns(i["l1_mix_post_norm_2"]))
    put("ssm_cw", columns(i["l1_ssm_conv_w_2"]))
    put("ssm_cb", columns(i["l1_ssm_conv_b_2"]))
    for name in ("dt_bias", "a_log"):
        out[:SH, PARAM[name][0]] = i[f"l1_{name}_2"]
    put("d_skip", columns(np.repeat(i["l1_d_skip_2"], HD)))
    put("gnorm", columns(i["l1_gate_norm_2"]))
    return out


def units(w):
    k, n = w.shape
    return w.reshape(k // P, P, n // 256, 256).transpose(2, 1, 0, 3).reshape(n // 256, P, -1)


def deep_units(w, parts):
    k, n = w.shape
    kt = k // P // parts
    return w.reshape(parts, kt, P, n // P, P).transpose(3, 0, 2, 1, 4).reshape(n // P * parts, P, kt * P)


def interleave(w):
    k, n = w.shape
    return w.reshape(k, 2, n // 256, P).transpose(0, 2, 1, 3).reshape(k, n)


def tokens(x):
    return x.reshape(-1, KT, P).transpose(2, 1, 0)


def lay_out(i):
    w = i["w_in"][0]
    cut = np.cumsum([0, 512, 512, 1024, 16, 1024, 1024, 1024, 1024, 1024, 1024])
    q, k, v, gates, o, dq, dk, dv, ga, gb = [w[:, cut[n]:cut[n + 1]] for n in range(10)]
    w0 = i["l0_w_in_2"]
    swap = np.arange(D).reshape(2, 8, HD).transpose(1, 0, 2).reshape(-1)
    w0 = np.concatenate([w0[:, :2 * D], w0[:, 2 * D:3 * D][:, swap], w0[:, 3 * D:]], axis=1)
    wo0 = np.concatenate([i["l0_w_out_2"][:D], i["l0_w_out_2"][D:][swap]], axis=0)
    w1 = i["l1_w_in_2"]
    merge = [units(ga), units(i["w_branch_a"][0]), units(gb), units(i["w_branch_b"][0])]
    out = {
        "xT": tokens(i["x"][0]), "ctxT": tokens(i["ctx"][0]), "metaT": tokens(i["meta_tokens_2"]),
        "params": pack_params(i), "consts": constants(),
        "w_ada": i["ada_w"][0].reshape(KT, P, 3, UW).transpose(2, 0, 1, 3).reshape(24, P, UW),
        "w_proj": np.concatenate([units(a) for a in (q, k, v, o, dq, dk, dv)]),
        "w_gates": gates.reshape(KT, P, 16).transpose(1, 0, 2),
        "w_merge": np.stack(merge, axis=1).reshape(16, P, -1),
        "w_out": units(i["w_out"][0]),
        "w_router": i["router_w"][0].reshape(KT, P, NE).transpose(1, 0, 2),
        "w_e1": i["exp_w1"][0].reshape(NE, KT, P, 2, 4, 2 * P).transpose(0, 1, 2, 4, 3, 5).reshape(NE, KT, P, -1),
        "w_e2": i["exp_w2"][0].reshape(NE, 4, 2, P, D).transpose(0, 1, 3, 2, 4).reshape(NE, 4, P, -1),
        "b2rows": i["exp_b2"][0],
        "w_l0": units(w0),
        "w_lru": np.stack([i["l0_lru_w_a_2"], i["l0_lru_w_x_2"]]).transpose(2, 0, 1, 3),
        "w_l0o": deep_units(wo0, 1),
        "w_l1": units(w1[:, :3 * DS]),
        "w_dt": w1[:, 3 * DS:].reshape(KT, P, SH).transpose(1, 0, 2),
        "w_l1o": deep_units(i["l1_w_out_2"], 1),
    }
    for n in (0, 1):
        out[f"w_up{n}"] = units(interleave(i[f"l{n}_ffn_w_up_2"]))
        out[f"w_down{n}"] = deep_units(i[f"l{n}_ffn_w_down_2"], 2)
    return {name: np.ascontiguousarray(a) for name, a in out.items()}


ARENA = 31744
LAST_PHASE = 20
MERGE0 = (48, 40, 64)


class Chain:

    def __init__(self, eng, sem):
        self.eng, self.sem, self.n = eng, sem, 0

    def __call__(self, ins):
        ins.then_inc(self.sem, 1)
        self.n += 1
        self.eng.wait_ge(self.sem, self.n)


class LoopChain:

    def __init__(self, eng, sem, i, per):
        self.eng, self.sem, self.i, self.per, self.n = eng, sem, i, per, 0

    def __call__(self, ins):
        ins.then_inc(self.sem, 1)
        self.n += 1
        self.eng.wait_ge(self.sem, self.i * self.per + self.n)

    def end(self):
        assert self.n == self.per, self.n


class Count:

    def __init__(self):
        self.unit = self.tile = self.out = self.norm = 0


def program(nc, dram, out):
    with ExitStack() as ctx:
        def sb(name, shape, dt=F32):
            return ctx.enter_context(nc.sbuf_tensor(name, shape, dt))

        sems = {}

        def sem(name):
            if name not in sems:
                sems[name] = ctx.enter_context(nc.semaphore(name))
            return sems[name]

        ring = sb("ring", [P, R, UW])
        par = sb("par", [P, NPARAM])
        con = sb("con", [P, NCONST])
        mod = sb("mod", [P, 48, 2])
        hT = sb("hT", [P, KT, L])
        arena = sb("arena", [P, ARENA])
        small = sb("small", [P, 512])
        bank = ctx.enter_context(nc.psum_tensor("bank", [P, 8, 512], F32))
        xT = hT[:, :, META:L]

        class Place:
            at, top = 0, 0

        def take(*shape, at=None):
            n = int(np.prod(shape))
            a = Place.at if at is None else at
            if at is None:
                Place.at += n
            Place.top = max(Place.top, a + n)
            assert a + n <= ARENA, (a + n, ARENA)
            v = arena[:, a:a + n]
            if len(shape) == 2:
                v = v.rearrange("p (a b) -> p a b", a=shape[0])
            if len(shape) == 3:
                v = v.rearrange("p (a b c) -> p a b c", a=shape[0], b=shape[1])
            return v

        def prm(name, a=0, n=1):
            at = PARAM[name][0] + a
            return par[:, at:at + n]

        def cst(name, a=0, n=None):
            at, size = CONST[name]
            return con[:, at + a:at + a + (size if n is None else n)]

        ident, ones = cst("ident"), cst("ones")

        stream = []
        for name, first, last in (("w_ada", 0, KT), ("w_proj", 0, 24), ("w_ada", KT, 3 * KT), ("w_merge", 0, 16),
                                  ("w_out", 0, 4)):
            stream += [(dram[name][n], UW) for n in range(first, last)]
        MOE0 = len(stream)
        EU = 12
        assert EU % R == 0
        tail = []
        for name in ("w_l0", "w_l0o", "w_up0", "w_down0", "w_l1", "w_l1o", "w_up1", "w_down1"):
            tail += [(dram[name][n], dram[name].shape[2]) for n in range(dram[name].shape[0])]
        TAIL0 = MOE0 + NE * EU
        NUNITS = TAIL0 + len(tail)

        def slot_filled(pe, at):
            u = at.unit
            pe.wait_ge(sem(f"filled{u % R}"), 16 * (u // R + 1))
            return u % R

        def out_bank(pe, at):
            b = at.out % NL
            if at.out >= NL:
                pe.wait_ge(sem(f"bank_read{b}"), at.out // NL)
            at.out += 1
            return bank[:, 6 + b, :]

        def tile_out(eng, at, last_in_unit):
            if last_in_unit:
                at.unit += 1
                eng.wait_ge(sem("unit_used"), at.unit)
            else:
                at.tile += 1
                eng.wait_ge(sem("tile_done"), at.tile)
            b = at.out % NL
            at.out += 1
            return bank[:, 6 + b, :], sem(f"bank_read{b}")

        def tile_skip(at, last_in_unit):
            if last_in_unit:
                at.unit += 1
            else:
                at.tile += 1
            at.out += 1

        def project(pe, at, n_units, rhs, n):
            for _ in range(n_units):
                s = slot_filled(pe, at)
                for c in range(2):
                    o = out_bank(pe, at)
                    for k in range(KT):
                        mm = pe.matmul(o[:, 0:n], ring[:, s, k * 256 + c * P:k * 256 + (c + 1) * P], rhs(k),
                                       start=(k == 0), stop=(k == KT - 1))
                    mm.then_inc(sem("tile_done") if c == 0 else sem("unit_used"), 1)
                at.unit += 1

        def project_tokens(pe, at, n_units, lhs, tiles):
            for _ in range(n_units):
                s = slot_filled(pe, at)
                for t in range(tiles):
                    o = out_bank(pe, at)
                    for k in range(KT):
                        mm = pe.matmul(o[:, 0:256], lhs(k, t), ring[:, s, k * 256:(k + 1) * 256],
                                       start=(k == 0), stop=(k == KT - 1))
                    mm.then_inc(sem("tile_done") if t < tiles - 1 else sem("unit_used"), 1)
                at.unit += 1

        def project_deep(pe, at, parts, kt, rhs, n, outs=KT):
            for _ in range(outs):
                o = out_bank(pe, at)
                for part in range(parts):
                    s = slot_filled(pe, at)
                    for k in range(kt):
                        mm = pe.matmul(o[:, 0:n], ring[:, s, k * P:(k + 1) * P], rhs(part * kt + k),
                                       start=(part == 0 and k == 0), stop=(part == parts - 1 and k == kt - 1))
                    mm.then_inc(sem("unit_used"), 1)
                    at.unit += 1

        NB_NORM = 5

        def norm_squares(act, src, dst, tiles=KT):
            for k in range(tiles):
                act.activation(dst(k), src(k), ACT.Square).then_inc(sem("squares"), 1)

        def norm_sums(pe, at, sq, n, tiles=KT):
            for k in range(tiles):
                pe.wait_ge(sem("squares"), at.norm + k + 1)
                mm = pe.matmul(bank[:, NB_NORM, 0:n], ones, sq(k), start=(k == 0), stop=(k == tiles - 1))
            at.norm += tiles
            mm.then_inc(sem("norm_sum"), 1)

        def norm_root(act, at, dst, n, width):
            at.norm += 1
            act.wait_ge(sem("norm_sum"), at.norm)
            act.activation(dst, bank[:, NB_NORM, 0:n], ACT.Sqrt, bias=cst("eps"), scale=1.0 / width)\
               .then_inc(sem("norm_root"), 1)

        def norm_inverse(dve, at, chain, rs):
            at.norm += 1
            dve.wait_ge(sem("norm_root"), at.norm)
            chain(dve.reciprocal(rs, rs))

        def phase(eng, n):
            eng.drain().then_inc(sem("phase"), 1)
            eng.wait_ge(sem("phase"), 4 * n)

        lat = slice(0, T)
        ada = take(2, 512, at=KT * 2 * T)
        u = take(KT, 2 * T)
        qm = take(4, T)
        km = take(4, 2 * T)
        vm_at = Place.at
        vm = take(4, D)
        og = take(KT, T)
        qd = take(NH_D, T)
        kd = take(NH_D, 2 * T)
        vd = take(4, D)
        aout = take(KT, T)
        work = Place.at
        ctxT = qd
        sq = vd
        bout = take(KT, T, at=vm_at)
        rs = small[:, :]
        tmp = small[:, :].rearrange("p (a b) -> p a b", a=2)
        crow = take(2, 2, T)
        rows = Place.at
        grow = take(2, 2, 2 * T)
        brow = take(2, 2 * T)
        arow = take(2, 2 * T)
        mrow = take(2, 2 * T)
        E2 = take(2, 4, T, at=rows)
        PM = take(2, 4, T, at=rows + 2048)
        emt = take(2, T, at=rows + 4096)
        dinv = take(T, at=rows + 4608)
        dabs = take(T, at=rows + 4864)
        cact = sb("cact", [P, 2 * KT, 16])
        ctmp = sb("ctmp", [P, 2 * KT])
        A1 = sb("A1", [P, 2, KT])
        A2 = sb("A2", [P, KT])
        gtok = sb("gtok", [P, 4, 16])
        gt1 = sb("gt1", [P, 4, 16])
        gt2 = sb("gt2", [P, 4, 16])
        gt3 = sb("gt3", [P, 4, 16])
        acol = sb("acol", [P, 2, 4, 4])
        lamc = sb("lamc", [P, 8])
        dg = sb("dg", [P, KT])
        mx = sb("mx", [P, 4])
        nm = sb("nm", [P, 2, 4])
        den = sb("den", [P, 2, 4])
        rden = sb("rden", [P, 4])
        PA = take(2, 4, 512, at=work)
        aT = take(4, T, at=work + 4096)
        rs8 = take(KT, T, at=work)
        sq8 = take(KT, T, at=work + 2048)
        sg = take(2, T, at=work)
        tmg = take(T, at=work + 512)
        y1 = qd

        Place.at = 0
        u2T = take(KT, T)
        u2tok = take(TT, D)
        sq2 = take(KT, T)
        actwarm = take(1)
        yacc = take(KT, T)
        rs2 = take(T)
        xe = take(KT, SLOTS)
        ht = take(3, 512)
        hg = take(2, 2, P)
        hl = take(2, 2, P)
        sgm = take(2, 2, P)
        actT = take(KT, SLOTS)
        ys = take(D)
        sel = take(TT, SLOTS)
        selg = take(TT, SLOTS)
        sgT = take(TT, P)
        b2r = take(D)
        gateT = take(T)
        lg = take(TT, NE)
        top = take(TT, 8)
        topf = take(TT, 8)
        chosen = take(TT, NE)
        ntop = take(TT)
        gsum = take(TT)
        gate = take(TT, NE + 2)
        place = take(TT, NE + 2)
        slots = take(SLOTS)
        topi = sb("topi", [P, TT, 8], U32)
        most_i = sb("most_i", [P, 1], I32)

        Place.at = 0
        ub = take(KT, L)
        sqb = take(KT, L)
        ym = take(KT, L)
        rsb = take(L)
        second = Place.at
        ga = take(KT, L)
        xr = take(KT, L + 3)
        xc = take(KT, L)
        rg = take(KT, L)
        ig = take(KT, L)
        wlru = take(2, 8, P)
        q0 = take(KT, L)
        k0 = take(L)
        v0 = take(3, P)
        mix = take(2 * KT, L)
        SC = (0, P, 3 * P)
        sc = take(3, 3 * P + L)
        pt = take(2, STRIP)
        th = sqb
        Place.at = second
        up = take(2, 2, L + 2)
        cv = take(2, 2, L)
        gl = take(2, L)
        actF = take(FT, L)
        Place.at = second
        zs = take(ST, L)
        xb = take(CT, L)
        xt = take(3, DS)
        dtr = take(L)
        csr = take(L)
        dt1 = take(L)
        dt2 = take(L)
        dt3 = take(L)
        strips = Place.at
        cbm = take(2, STRIP)
        dec = take(2, STRIP)
        wts = take(2, STRIP)
        xp = take(4, L + 3, at=strips)
        xv = take(4, L, at=strips + 4 * (L + 3))
        sq16 = take(ST, L, at=second + ST * L)
        rs16 = take(SG, L, at=second + 2 * ST * L)
        smx = sb("smx", [P, 2, 3])
        snm = sb("snm", [P, 2, 3])
        sden = sb("sden", [P, 2, 3])
        ssk = sb("ssk", [P, 2, 3])
        lru1 = sb("lru1", [P, KT])
        lru2 = sb("lru2", [P, KT])
        lru3 = sb("lru3", [P, KT])
        nlru = sb("nlru", [P, KT])
        dtc = sb("dtc", [P, 3, SH])
        csc = sb("csc", [P, 3, SH])
        acl = sb("acl", [P, 2])

        wg = sb("wg", [P, KT, 16])
        wr = sb("wr", [P, KT, NE])
        wdt = sb("wdt", [P, KT, SH])

        block = ctx.enter_context(nc.Block())

        @block.sync
        def _(sp):
            def fill(n, src, width):
                if n >= R:
                    sp.wait_ge(sem("unit_used"), n - R + 1)
                sp.dma_start(ring[:, n % R, 0:width], src).then_inc(sem(f"filled{n % R}"), 16)

            for n, (src, width) in enumerate(stream):
                fill(n, src, width)

            def fill_experts(i, e, filled, used, u0, used0):
                for j in range(EU):
                    s = (u0 + j) % R
                    sp.wait_ge(sem(used), i * EU + (used0 + j - R + 1))
                    name, c = ("w_e1", j) if j < KT else ("w_e2", j - KT)
                    sp.dma_start(ring[:, s, :], dram[name][bass.ds(e, 1), c, :, :].rearrange("a p n -> (a p) n"))\
                      .then_inc(sem(f"{filled}{s}"), 16)

            with sp.Fori(0, NE) as e:
                fill_experts(e, e, "filled", "unit_used", MOE0, MOE0)
            sp.wait_ge(sem("most_known"), 1)
            most = sp.value_load(most_i[0:1, 0:1], min_val=0, max_val=T)
            sp.wait_ge(sem("unit_used"), TAIL0)
            with sp.If(most > SLOTS):
                sp.nop().then_inc(sem("more_used"), R)
                with sp.Fori(0, PASSES - 1) as b:
                    with sp.Fori(0, NE) as e:
                        fill_experts(b * NE + e, e, "more_filled", "more_used", 0, R)
                sp.wait_ge(sem("more_used"), R + (PASSES - 1) * NE * EU)
            with sp.Else():
                sp.nop()
            for n, (src, width) in enumerate(tail):
                fill(TAIL0 + n, src, width)
            sp.wait_ge(sem("phase"), 4 * LAST_PHASE)
            sp.dma_start(out, xT).then_inc(sem("stored"), 16)
            sp.wait_ge(sem("stored"), 16)

        @block.scalar
        def _(act):
            at = Count()
            chain = Chain(act, sem("act_chain"))
            act.dma_start(par[:, :], dram["params"]).then_inc(sem("par_loaded"), 16)
            act.dma_start(xT, dram["xT"]).then_inc(sem("x_loaded"), 16)
            act.dma_start(ctxT[:, :, :], dram["ctxT"]).then_inc(sem("x_loaded"), 16)
            act.dma_start(con[:, :], dram["consts"]).then_inc(sem("con_loaded"), 16)
            act.dma_start(wg[:, :, :], dram["w_gates"]).then_inc(sem("con_loaded"), 16)
            act.dma_start(wr[:, :, :], dram["w_router"]).then_inc(sem("con_loaded"), 16)
            act.dma_start(wdt[:, :, :], dram["w_dt"]).then_inc(sem("con_loaded"), 16)
            act.dma_start(hT[:, :, 0:META], dram["metaT"]).then_inc(sem("con_loaded"), 16)

            act.wait_ge(sem("par_loaded"), 16)
            act.activation(cact[:, :, :], prm("c", 0, 16).unsqueeze(2).to_broadcast([P, 16, 16]), ACT.Silu).then_inc(sem("c_ready"), 1)
            act.wait_ge(sem("x_loaded"), 32)
            for k in range(KT):
                act.activation(sq.rearrange("p a (b c) -> p (a b) c", c=512)[:, k, 0:T], xT[:, k, :], ACT.Square)
                act.activation(sq.rearrange("p a (b c) -> p (a b) c", c=512)[:, k, T:2 * T], ctxT[:, k, :],
                               ACT.Square).then_inc(sem("squares"), 1)
            act.wait_ge(sem("con_loaded"), 80)
            norm_root(act, at, rs, 512, D)
            act.wait_ge(sem("unit_used"), KT)
            act.activation(ada[:, 0, :], bank[:, 6, :], ACT.Copy).then_inc(sem("ada_copied"), 1)
            at.unit = KT
            for k in range(KT):
                act.wait_ge(sem("u_scaled"), k + 1)
                act.activation(u[:, k, lat], u[:, k, lat], ACT.Identity, bias=mod[:, k, 0:1])
                act.activation(u[:, k, T:2 * T], u[:, k, T:2 * T], ACT.Identity, bias=mod[:, k, 1:2])\
                   .then_inc(sem("u_ready"), 1)

            def copy_tiles(n_units, dst, width, func=ACT.Copy):
                for n in range(2 * n_units):
                    o, free = tile_out(act, at, n % 2 == 1)
                    act.activation(dst(n), o[:, 0:width], func).then_inc(free, 1)

            def copy_tokens(n_units, dst):
                for n in range(n_units):
                    for t in range(4):
                        o, free = tile_out(act, at, t == 3)
                        act.activation(dst[:, t, n * 256:(n + 1) * 256], o[:, 0:256], ACT.Copy).then_inc(free, 1)

            copy_tiles(2, lambda n: qm[:, n, :], T)
            copy_tiles(2, lambda n: km[:, n, :], 2 * T)
            act.wait_ge(sem("gates_biased"), 1)
            chain(act.activation(gt1[:, :, :], gtok[:, :, :], ACT.Abs))
            act.activation(gt1[:, :, :], gt1[:, :, :], ACT.Exp, scale=-1.0).then_inc(sem("gate_exp"), 1)
            copy_tokens(4, vm)
            act.wait_ge(sem("gates_turned"), 1)
            for d in range(2):
                for kind in range(2):
                    ins = act.activation(grow[0:4, d, kind, :], bank[0:4, 2 * d + kind, :], ACT.Copy)
            ins.then_inc(sem("grow_ready"), 1)
            copy_tiles(4, lambda n: og[:, n, :], T, ACT.Sigmoid)
            copy_tiles(4, lambda n: qd[:, n, :], T)
            act.wait_ge(sem("acol_turned"), 1)
            act.activation(acol[:, :, :, :], bank[:, 4, 0:32].rearrange("p (a b c) -> p a b c", a=2, b=4),
                           ACT.Copy).then_inc(sem("acol_ready"), 1)
            copy_tiles(4, lambda n: kd[:, n, :], 2 * T)
            copy_tokens(4, vd)

            def decay(i):
                act.wait_ge(sem("arg_ready"), i + 1)
                if i >= 2:
                    act.wait_ge(sem("m_fin"), i - 1)
                act.activation(E2[:, i % 2, :, :], E2[:, i % 2, :, :], ACT.Exp)
                act.activation(emt[:, i % 2, :], bank[:, 2 + i % 2, T:2 * T], ACT.Exp).then_inc(sem("decay_ready"), 1)

            decay(0)
            for i in range(8):
                if i < 7:
                    decay(i + 1)
                act.wait_ge(sem("m_sums"), i + 1)
                act.activation(dabs, bank[:, 5, 0:T], ACT.Abs).then_inc(sem("dabs_ready"), 1)
            at.unit += 2 * KT
            phase(act, 1)
            act.activation(ada[:, :, :], bank[:, 6:8, :], ACT.Copy).then_inc(sem("ada_copied"), 1)
            norm_squares(act, lambda k: aout[:, k, :], lambda k: sq8[:, k, :])
            act.wait_ge(sem("head_sums"), 1)
            act.activation(rs8[:, 0:4, :], bank[:, 0:2, :].rearrange("p a (b c) -> p (a b) c", c=T), ACT.Sqrt,
                           bias=cst("eps"), scale=1.0 / DV_M).then_inc(sem("head_root"), 1)
            phase(act, 2)
            act.wait_ge(sem("lambda_step"), 2)
            act.activation(lamc[:, 2:4], bank[:, 4, 0:2], ACT.Exp).then_inc(sem("lambda_step"), 1)

            def head_out(h):
                act.wait_ge(sem("d_out"), h + 1)
                act.activation(bout[:, h, :], bank[:, 6 + h % 2, 0:T], ACT.Copy).then_inc(sem("bout_ready"), 1)

            for h in range(NH_D):
                if h >= 2:
                    act.wait_ge(sem("a_turned"), 2 * (h - 1))
                for j in range(4):
                    act.wait_ge(sem("negmax"), 4 * h + j + 1)
                    act.activation(PA[:, h % 2, j, :], bank[:, j, :], ACT.Exp, bias=nm[:, h % 2, j:j + 1],
                                   scale=DH_D ** -0.5, accum_out=den[:, h % 2, j:j + 1]).then_inc(sem("probs"), 1)
                if h >= 1:
                    head_out(h - 1)
                for qt in range(2):
                    act.wait_ge(sem("a_turned"), 2 * h + qt + 1)
                    act.activation(aT[:, :, qt * P:(qt + 1) * P],
                                   bank[:, 4 + qt, :].rearrange("p (a b) -> p a b", a=4), ACT.Copy)\
                       .then_inc(sem("aT_ready"), 1)
            head_out(NH_D - 1)
            phase(act, 3)
            act.wait_ge(sem("bout_ready"), NH_D)
            norm_squares(act, lambda k: bout[:, k, :], lambda k: sq8[:, k, :])
            act.wait_ge(sem("head_sums"), 2)
            act.activation(rs8[:, :, :], bank[:, 0:4, :].rearrange("p a (b c) -> p (a b) c", c=T), ACT.Sqrt,
                           bias=cst("eps"), scale=1.0 / (2 * DH_D)).then_inc(sem("head_root"), 1)
            phase(act, 4)
            for p in range(4):
                for branch in range(2):
                    for c in range(2):
                        o, free = tile_out(act, at, c == 1)
                        act.activation(sg[:, c, :], o[:, 0:T], ACT.Sigmoid).then_inc(free, 1)
                    for c in range(2):
                        tile_skip(at, c == 1)
            for c in range(8):
                tile_skip(at, c % 2 == 1)
            phase(act, 5)
            norm_squares(act, lambda k: xT[:, k, :], lambda k: sq2[:, k, :])
            norm_root(act, at, rs2, T, D)
            for k in range(KT):
                act.wait_ge(sem("u2_scaled"), k + 1)
                act.activation(u2T[:, k, :], u2T[:, k, :], ACT.Identity, bias=mod[:, 24 + k, 0:1])\
                   .then_inc(sem("u2_ready"), 1)
            for t in range(TT):
                for b in range(2):
                    act.wait_ge(sem("u2_turned"), 2 * t + b + 1)
                    act.activation(u2tok[:, t, b * 512:(b + 1) * 512], bank[:, 2 * t + b, :], ACT.Copy)\
                       .then_inc(sem("u2tok_ready"), 1)
            for t in range(TT):
                act.wait_ge(sem("top_negated"), t + 1)
                act.activation(gate[:, t, 1:NE + 1], lg[:, t, :], ACT.Exp, bias=ntop[:, t:t + 1])\
                   .then_inc(sem("gate_exps"), 1)
            act.wait_ge(sem("gate_turned"), 1)
            act.activation(gateT[0:NE, :], bank[0:NE, 6, 0:T], ACT.Copy).then_inc(sem("gateT_ready"), 1)
            phase(act, 6)

            def gathered(n, x):
                act.wait_ge(sem(x + "gathered"), n)
                for b in range(2):
                    ins = act.activation(xe[:, 4 * b:4 * b + 4, :],
                                         bank[:, 4 + b, 0:4 * SLOTS].rearrange("p (a b) -> p a b", a=4), ACT.Copy)
                ins.then_inc(sem(x + "xe_ready"), 1)

            def gates_turned(n, x):
                act.wait_ge(sem(x + "sg_turned"), n)
                act.activation(sgT[0:SLOTS, :, :], bank[0:SLOTS, 4, 0:T], ACT.Copy).then_inc(sem(x + "sgT_ready"), 1)

            def expert_act(i, m, e, used, u0, x):
                act.activation(actwarm[:, 0:1], ones[:, 0:1], ACT.Sigmoid)
                gates_turned(m + 1, x)
                act.wait_ge(sem(x + "w1_round"), i * 2 + 1)
                act.activation(ht[:, 0, :], bank[:, 0, :], ACT.Copy).then_inc(sem(x + "ht_ready"), 1)
                act.wait_ge(sem(used), i * EU + (u0 + KT))
                act.activation(ht[:, 2, :], bank[:, 2, :], ACT.Copy).then_inc(sem(x + "ht_ready"), 1)
                for r in range(3):
                    if r == 2:
                        act.wait_ge(sem(x + "act_ready"), i * 3 + 1)
                    act.wait_ge(sem(x + "h_turned"), i * 3 + (r + 1))
                    for q, b, g, n in pieces(ROUNDS[r]):
                        for c in range(2):
                            ins = act.activation(hl[:, r % 2, c, q * GROUP:(q + n) * GROUP],
                                                 bank[:, LINEAR_BANKS[r], c * P + q * GROUP:c * P + (q + n) * GROUP],
                                                 ACT.Identity,
                                                 bias=par[:, bass.ds(e * 16 + (PARAM["b1"][0] + 4 * b + 2 + c), 1)])
                    ins.then_inc(sem(x + "linear_biased"), 1)
                    act.wait_ge(sem(x + "biased"), i * 3 + (r + 1))
                    act.activation(sgm[:, r % 2, :, :], hg[:, r % 2, :, :], ACT.Sigmoid, scale=ALPHA)\
                       .then_inc(sem(x + "sig_ready"), 1)
                gathered(m + 2, x)
                act.wait_ge(sem(used), i * EU + (u0 + EU))
                for r, tasks in enumerate(ROUNDS):
                    y = bank[:, 6 + r // 2, (r % 2) * 256:(r % 2 + 1) * 256]
                    for q, b, g, n in pieces(tasks):
                        for j, w in ((0, n),) if q == 0 and g == 0 else [(j, 1) for j in range(n)]:
                            ins = act.activation(ys[(g + j) * GROUP:(g + j + w) * GROUP, b * 256:(b + 1) * 256],
                                                 y[(q + j) * GROUP:(q + j + w) * GROUP, :], ACT.Copy)
                ins.then_inc(sem(x + "ys_ready"), 1)

            gathered(1, "")
            with act.Fori(0, NE) as e:
                expert_act(e, e, e, "unit_used", MOE0, "")
            gates_turned(NE + 1, "")
            phase(act, 7)
            most = act.value_load(most_i[0:1, 0:1], min_val=0, max_val=T)
            with act.If(most > SLOTS):
                act.nop().then_inc(sem("more_ys_ready"), 1)
                with act.Fori(0, PASSES - 1) as b:
                    gathered(b * (NE + 1) + 1, "more_")
                    with act.Fori(0, NE) as e:
                        expert_act(b * NE + e, b * (NE + 1) + e, e, "more_used", R, "more_")
                    gates_turned(b * (NE + 1) + (NE + 1), "more_")
            with act.Else():
                act.nop()
            phase(act, 8)
            act.wait_ge(sem("x2_ready"), 1)
            norm_squares(act, lambda k: xT[:, k, :], lambda k: sq2[:, k, :])
            norm_root(act, at, rs2, T, D)
            phase(act, 9)
            at.unit = TAIL0

            def pre_norm():
                norm_squares(act, lambda k: hT[:, k, :], lambda k: sqb[:, k, :])
                norm_root(act, at, rsb, L, D)

            def result_tiles(parts):
                for k in range(KT):
                    for _ in range(parts - 1):
                        at.unit += 1
                    o, free = tile_out(act, at, True)
                    act.activation(sqb[:, k, :], o[:, 0:L], ACT.Square).then_inc(sem("squares"), 1)
                    act.activation(ym[:, k, :], o[:, 0:L], ACT.Copy).then_inc(free, 1)
                norm_root(act, at, rsb, L, D)

            def ffn():
                pre_norm()
                for j in range(FT):
                    if j >= 2:
                        act.wait_ge(sem("ffn_conv"), at.ffn + j - 1)
                    for c in range(2):
                        o, free = tile_out(act, at, c == 1)
                        act.activation(up[:, j % 2, c, 2:], o[:, 0:L], ACT.Copy).then_inc(free, 1)
                    if j >= 1:
                        ffn_gelu(j - 1)
                ffn_gelu(FT - 1)
                at.ffn += FT

            def ffn_gelu(j):
                act.wait_ge(sem("ffn_conv"), at.ffn + j + 1)
                act.activation(gl[:, j % 2, :], cv[:, j % 2, 0, :], ACT.Gelu_apprx_tanh).then_inc(sem("ffn_gelu"), 1)

            at.ffn = 0
            act.dma_start(wlru[:, :, :, :], dram["w_lru"]).then_inc(sem("lru_loaded"), 16)
            pre_norm()
            chain(act.activation(lru1[:, :], prm("lru_lam", 0, 8), ACT.Abs))
            act.activation(lru1[:, :], lru1[:, :], ACT.Exp, scale=-1.0).then_inc(sem("lam_exps"), 1)
            for n in range(8):
                o, free = tile_out(act, at, n % 2 == 1)
                act.activation(ga[:, n, :], o[:, 0:L], ACT.Gelu_apprx_tanh).then_inc(free, 1)
            for n in range(8):
                o, free = tile_out(act, at, n % 2 == 1)
                act.activation(xr[:, n, 3:], o[:, 0:L], ACT.Copy).then_inc(free, 1)
            for n in range(8):
                o, free = tile_out(act, at, n % 2 == 1)
                act.activation(q0[:, n, :], o[:, 0:L], ACT.Copy).then_inc(free, 1)
            o, free = tile_out(act, at, False)
            act.activation(k0, o[:, 0:L], ACT.Copy).then_inc(free, 1)
            o, free = tile_out(act, at, True)
            act.activation(v0[:, 0:2, :], o[:, 0:2 * P].rearrange("p (a b) -> p a b", a=2), ACT.Copy)
            act.activation(v0[0:META, 2, :], o[0:META, 2 * P:3 * P], ACT.Copy).then_inc(free, 1)
            for n in range(8):
                act.wait_ge(sem("lru_gates"), n + 1)
                b = 2 * (n % 2)
                act.activation(rg[:, n, :], bank[:, b, 0:L], ACT.Sigmoid, bias=prm("lru_ba", n))
                act.activation(ig[:, n, :], bank[:, b + 1, 0:L], ACT.Sigmoid, bias=prm("lru_bx", n))\
                   .then_inc(sem("lru_gate_read"), 1)
            act.wait_ge(sem("lru_gate_read"), 8)
            act.wait_ge(sem("nlru_ready"), 1)
            for n in range(8):
                act.activation(th[:, n, :], rg[:, n, :], ACT.Tanh, scale=lru2[:, n:n + 1]).then_inc(sem("lru_tanh"), 1)
            act.wait_ge(sem("lru_tanh"), 8)
            for n in range(8):
                act.activation(rg[:, n, :], rg[:, n, :], ACT.Exp, scale=nlru[:, n:n + 1]).then_inc(sem("lru_decay"), 1)
            phase(act, 10)

            def swa_out(i):
                act.wait_ge(sem("swa_turned"), i + 1)
                if i >= 2:
                    act.wait_ge(sem("swa_pv"), i - 1)
                act.activation(pt[:, i % 2, 0:SEG[2]], bank[:, 6, 0:SEG[2]], ACT.Copy)
                act.activation(pt[0:META, i % 2, SEG[2]:], bank[0:META, 6, SEG[2]:STRIP], ACT.Copy)\
                   .then_inc(sem("pt_ready"), 1)
                if i % 2 == 1:
                    act.wait_ge(sem("swa_pv"), i + 1)
                    act.activation(mix[:, 8 + i // 2, :], bank[:, 7, 0:L], ACT.Copy).then_inc(sem("swa_result"), 1)

            for i in range(HEADS2):
                if i == 8:
                    act.wait_ge(sem("lru_ratio"), 8)
                    act.activation(th[:, :, :], th[:, :, :], ACT.Sqrt, scale=2.0).then_inc(sem("lru_root"), 1)
                act.wait_ge(sem("swa_negmax"), i + 1)
                b = i % 2
                for t, (t0, n) in enumerate(TOK):
                    s = sc[0:n, i % 3, SC[t]:SC[t] + t0 + n]
                    act.activation(s, s, ACT.Exp, bias=snm[0:n, b, t:t + 1],
                                   scale=HD ** -0.5, accum_out=sden[0:n, b, t:t + 1])
                act.activation(ssk[:, b, :], snm[:, b, :], ACT.Exp, bias=prm("sinks", i)).then_inc(sem("swa_exp"), 1)
                if i >= 1:
                    swa_out(i - 1)
            swa_out(HEADS2 - 1)
            phase(act, 11)
            result_tiles(1)
            phase(act, 12)
            ffn()
            result_tiles(2)
            phase(act, 13)
            phase(act, 14)
            pre_norm()
            for n in range(ST):
                o, free = tile_out(act, at, n % 2 == 1)
                act.activation(zs[:, n, :], o[:, 0:L], ACT.Silu).then_inc(free, 1)

            def conv_silu(n):
                act.wait_ge(sem("ssm_conv"), n + 1)
                act.activation(xb[:, n, :], xv[:, n % 4, :], ACT.Silu).then_inc(sem("ssm_silu"), 1)

            for n in range(CT):
                o, free = tile_out(act, at, n % 2 == 1)
                if n >= 4:
                    act.wait_ge(sem("ssm_conv"), n - 3)
                act.activation(xp[:, n % 4, 3:], o[:, 0:L], ACT.Copy).then_inc(free, 1)
                if n >= 2:
                    conv_silu(n - 2)
            conv_silu(CT - 2)
            conv_silu(CT - 1)
            act.wait_ge(sem("dt_step"), 2)
            act.activation(acl[0:SH, 0:1], prm("a_log")[0:SH, :], ACT.Exp)
            chain(act.activation(dt1[0:SH, :], dtr[0:SH, :], ACT.Abs))
            act.activation(dt1[0:SH, :], dt1[0:SH, :], ACT.Exp, scale=-1.0).then_inc(sem("dt_step"), 1)
            phase(act, 15)
            for b in range(8):
                t = b // 4
                act.wait_ge(sem("x_turned"), b + 1)
                act.activation(xt[:, t, (b % 4) * 512:(b % 4 + 1) * 512], bank[:, b % 2, :], ACT.Copy)\
                   .then_inc(sem("x_turn_read"), 1)
            for b in range(8, 12):
                act.wait_ge(sem("x_turned"), b + 1)
                act.activation(xt[0:META, 2, (b % 4) * 512:(b % 4 + 1) * 512], bank[0:META, b % 2, :], ACT.Copy)\
                   .then_inc(sem("x_turn_read"), 1)
            act.wait_ge(sem("dt_turned"), 1)
            for c, (t0, n) in enumerate(TOK):
                act.activation(csc[0:n, c, :], bank[0:n, 2, c * 64:c * 64 + SH], ACT.Copy, scale=-1.0)
                act.activation(dtc[0:n, c, :], bank[0:n, 2, c * 64 + SH:c * 64 + 2 * SH], ACT.Copy)
            phase(act, 16)
            for h in range(SH):
                act.wait_ge(sem("ssm_args"), h + 1)
                act.activation(dec[:, h % 2, 0:SEG[2]], dec[:, h % 2, 0:SEG[2]], ACT.Exp)
                act.activation(dec[0:META, h % 2, SEG[2]:], dec[0:META, h % 2, SEG[2]:], ACT.Exp)\
                   .then_inc(sem("ssm_decay"), 1)
            phase(act, 17)
            norm_squares(act, lambda k: zs[:, k, :], lambda k: sq16[:, k, :], ST)
            for g in range(SG):
                act.wait_ge(sem("group_sums"), g + 1)
                act.activation(rs16[:, g, :], bank[:, g, 0:L], ACT.Sqrt, bias=cst("eps"), scale=1.0 / (DS // SG))\
                   .then_inc(sem("group_root"), 1)
            phase(act, 18)
            result_tiles(1)
            phase(act, 19)
            ffn()
            result_tiles(2)
            phase(act, 20)

        @block.vector
        def _(dve):
            at = Count()
            chain = Chain(dve, sem("dve_chain"))
            dve.wait_ge(sem("con_loaded"), 80)
            dve.wait_ge(sem("par_loaded"), 16)
            norm_inverse(dve, at, chain, rs)

            def modulation(g, b):
                dve.wait_ge(sem("ada_turned"), g + 1)
                turned = bank[:, b, :].rearrange("p (c q j x) -> p c q j x", c=4, q=4, j=2)
                out = mod[:, 16 * g:16 * (g + 1), :].rearrange("p (q c) j -> p q c j", q=4)
                bias = prm("ada_b", 16 * g, 16).rearrange("p (q c) -> p q c", q=4)
                for j in range(2):
                    ins = dve.tensor_tensor(out[:, :, :, j], turned[:, :, :, j, 0].rearrange("p c q -> p q c"), bias, ALU.add)
                chain(ins)

            modulation(0, 7)
            chain(dve.tensor_scalar(dg[:, :], prm("dnorm_g", 0, 8), 1.0 - LAM_INIT, None, ALU.mult))
            for j in range(2):
                chain(dve.scalar_tensor_tensor(out=A1[:, j, :], in0=mod[:, 8:16, j], scalar=1.0,
                                               in1=prm("norm1_g", 0, 8), op0=ALU.add, op1=ALU.mult))
            for k in range(KT):
                dve.scalar_tensor_tensor(out=u[:, k, lat], in0=xT[:, k, :], scalar=A1[:, 0, k:k + 1],
                                         in1=rs[:, lat], op0=ALU.mult, op1=ALU.mult)
                dve.scalar_tensor_tensor(out=u[:, k, T:2 * T], in0=ctxT[:, k, :], scalar=A1[:, 1, k:k + 1],
                                         in1=rs[:, T:2 * T], op0=ALU.mult, op1=ALU.mult).then_inc(sem("u_scaled"), 1)

            dve.wait_ge(sem("gates_done"), 1)
            for t in range(4):
                ins = dve.tensor_tensor(gtok[:, t, :], bank[:, 4, t * 16:(t + 1) * 16], prm("gate_b", 0, 16), ALU.add)
            ins.then_inc(sem("gates_biased"), 1)
            dve.wait_ge(sem("gate_exp"), 1)
            log1p(dve, chain, gt1[:, :, :], gt2[:, :, :], gt3[:, :, :])
            for d in range(2):
                chain(dve.scalar_tensor_tensor(out=gtok[:, :, 8 * d + 4:8 * d + 8], in0=gtok[:, :, 8 * d + 4:8 * d + 8],
                                               scalar=0.0, in1=gt1[:, :, 8 * d + 4:8 * d + 8],
                                               op0=ALU.min, op1=ALU.subtract))
            dve.memset(mrow[0:4, :, :], 0.0).then_inc(sem("logf_ready"), 1)
            dve.wait_ge(sem("grow_ready"), 1)
            for d in range(2):
                for part, init in ((1, None), (0, T)):
                    a0 = part * T
                    seg = slice(a0, a0 + T) if d == 0 else slice(a0 + T - 1, a0 - 1 if a0 else None, -1)
                    prev = (2 * T - 1) if d == 0 else T
                    chain(dve.tensor_tensor_scan(out=brow[0:4, d, seg], data0=grow[0:4, d, 1, seg],
                                                 data1=mrow[0:4, 1, 0:T],
                                                 initial=0.0 if part else brow[0:4, d, prev:prev + 1],
                                                 op0=ALU.add, op1=ALU.add))
            chain(dve.tensor_tensor(arow[0:4, :, :], grow[0:4, :, 0, :], brow[0:4, :, :], ALU.subtract))
            for d in range(2):
                for part in (1, 0):
                    a0 = part * T
                    seg = slice(a0, a0 + T) if d == 0 else slice(a0 + T - 1, a0 - 1 if a0 else None, -1)
                    prev = (2 * T - 1) if d == 0 else T
                    chain(dve.tensor_tensor_scan(out=mrow[0:4, d, seg], data0=arow[0:4, d, seg],
                                                 data1=arow[0:4, d, seg],
                                                 initial=0.0 if part else mrow[0:4, d, prev:prev + 1],
                                                 op0=ALU.max, op1=ALU.max))
            chain(dve.tensor_scalar(crow[0:4, :, 0, :], mrow[0:4, :, 0:T], -1.0, None, ALU.mult))
            dve.tensor_tensor(crow[0:4, :, 1, :], crow[0:4, :, 0, :], brow[0:4, :, 0:T], ALU.subtract)\
               .then_inc(sem("rows_ready"), 1)

            def decay_args(i):
                h, d = i // 2, i % 2
                dve.wait_ge(sem("m_rows"), i + 1)
                for c in range(4):
                    ins = dve.tensor_scalar(E2[:, i % 2, c, :], bank[:, 2 + i % 2, 0:T], acol[:, d, c, h:h + 1], 0.0,
                                            ALU.add, ALU.min)
                ins.then_inc(sem("arg_ready"), 1)

            def weights(i):
                dve.wait_ge(sem("decay_ready"), i + 1)
                mask = cst("mask", (i % 2) * 512, 512).rearrange("p (a b) -> p a b", a=2)
                chain(dve.tensor_tensor(E2[:, i % 2, 0:2, :], E2[:, i % 2, 0:2, :], mask, ALU.mult))
                if i >= 2:
                    dve.wait_ge(sem("m_sums"), i - 1)
                for b in range(2):
                    ins = dve.scalar_tensor_tensor(
                        out=PM[:, i % 2, 2 * b:2 * b + 2, :], in0=bank[:, b, :].rearrange("p (a b) -> p a b", a=2),
                        scalar=P ** -0.5, in1=E2[:, i % 2, 2 * b:2 * b + 2, :], op0=ALU.mult, op1=ALU.mult)
                ins.then_inc(sem("m_weights"), 1)

            def divide(i):
                h, d = i // 2, i % 2
                dve.wait_ge(sem("dabs_ready"), i + 1)
                chain(dve.tensor_tensor(dinv, dabs, emt[:, i % 2, :], ALU.max))
                chain(dve.reciprocal(dinv, dinv))
                for j in range(2):
                    dst = aout[:, 2 * h + j, :] if d == 0 else tmp[:, j, :]
                    ins = dve.tensor_tensor(dst, bank[:, 4, j * T:(j + 1) * T], dinv, ALU.mult)
                ins.then_inc(sem("m_fin"), 1)
                dve.wait_ge(sem("m_fin"), i + 1)
                if d == 1:
                    chain(dve.tensor_tensor(aout[:, 2 * h:2 * h + 2, :], aout[:, 2 * h:2 * h + 2, :], tmp, ALU.add))

            dve.wait_ge(sem("acol_ready"), 1)
            decay_args(0)
            for i in range(8):
                if i < 7:
                    decay_args(i + 1)
                weights(i)
                if i > 0:
                    divide(i - 1)
            divide(7)
            for n in range(2 * NH_D):
                x = qd[:, n, :] if n < NH_D else kd[:, n - NH_D, lat]
                dve.wait_ge(sem("rotated"), n + 1)
                dve.tensor_tensor(tmp[:, 0, :], bank[:, 2 + n % 2, 0:T], cst("sin"), ALU.mult)\
                   .then_inc(sem("rot_read"), 1)
                chain(dve.tensor_tensor(x, x, cst("cos"), ALU.mult))
                dve.wait_ge(sem("rot_read"), n + 1)
                chain(dve.tensor_tensor(x, x, tmp[:, 0, :], ALU.add))
            phase(dve, 1)
            modulation(1, 2)
            modulation(2, 3)
            chain(dve.scalar_tensor_tensor(out=A2[:, :], in0=mod[:, 32:40, 0], scalar=1.0,
                                           in1=prm("norm2_g", 0, 8), op0=ALU.add, op1=ALU.mult))
            dve.wait_ge(sem("head_root"), 1)
            chain(dve.reciprocal(rs8[:, 0:4, :], rs8[:, 0:4, :]))
            for k in range(KT):
                ins = dve.scalar_tensor_tensor(out=aout[:, k, :], in0=aout[:, k, :], scalar=prm("mnorm_g", k),
                                               in1=rs8[:, k // 2, :], op0=ALU.mult, op1=ALU.mult)
            chain(ins)
            chain(dve.tensor_tensor(aout[:, :, :], aout[:, :, :], og[:, :, :], ALU.mult))
            for j in range(2):
                ins = dve.tensor_tensor(lamc[:, j:j + 1], prm("lam_p", 2 * j), prm("lam_p", 2 * j + 1), ALU.mult)
            ins.then_inc(sem("lambda_step"), 1)
            phase(dve, 2)
            dve.wait_ge(sem("lambda_step"), 3)
            chain(dve.tensor_tensor(lamc[:, 4:5], lamc[:, 3:4], lamc[:, 2:3], ALU.subtract))
            chain(dve.tensor_scalar(lamc[:, 5:6], lamc[:, 4:5], -LAM_INIT, None, ALU.add))
            for h in range(NH_D):
                for j in range(4):
                    dve.wait_ge(sem("scores"), 4 * h + j + 1)
                    chain(dve.reduce_max(mx[:, j:j + 1], bank[:, j, :], AX_X))
                    dve.tensor_scalar(nm[:, h % 2, j:j + 1], mx[:, j:j + 1], -DH_D ** -0.5, None, ALU.mult)\
                       .then_inc(sem("negmax"), 1)
                dve.wait_ge(sem("probs"), 4 * h + 4)
                chain(dve.reciprocal(rden[:, :], den[:, h % 2, :]))
                chain(dve.tensor_scalar(rden[:, 2:4], rden[:, 2:4], lamc[:, 5:6], None, ALU.mult))
                for qt in range(2):
                    chain(dve.tensor_scalar(PA[:, h % 2, qt, :], PA[:, h % 2, qt, :], rden[:, qt:qt + 1], None, ALU.mult))
                    dve.scalar_tensor_tensor(out=PA[:, h % 2, qt, :], in0=PA[:, h % 2, 2 + qt, :],
                                             scalar=rden[:, 2 + qt:3 + qt], in1=PA[:, h % 2, qt, :],
                                             op0=ALU.mult, op1=ALU.add).then_inc(sem("a_ready"), 1)
            phase(dve, 3)
            dve.wait_ge(sem("head_root"), 2)
            chain(dve.reciprocal(rs8[:, :, :], rs8[:, :, :]))
            for k in range(KT):
                ins = dve.scalar_tensor_tensor(out=bout[:, k, :], in0=bout[:, k, :], scalar=dg[:, k:k + 1],
                                               in1=rs8[:, k, :], op0=ALU.mult, op1=ALU.mult)
            phase(dve, 4)
            at.unit, at.tile, at.out = MERGE0
            for p in range(4):
                for branch in range(2):
                    for c in range(2):
                        tile_skip(at, c == 1)
                    for c in range(2):
                        o, free = tile_out(dve, at, c == 1)
                        y = y1[:, 2 * p + c, :]
                        if branch == 0:
                            dve.tensor_tensor(y, o[:, 0:T], sg[:, c, :], ALU.mult).then_inc(free, 1)
                        else:
                            dve.tensor_tensor(tmg, o[:, 0:T], sg[:, c, :], ALU.mult).then_inc(free, 1)
                            dve.wait_ge(free, (at.out + 1) // NL)
                            chain(dve.tensor_tensor(y, y, tmg, ALU.add))
            dve.drain().then_inc(sem("merged"), 1)
            for k in range(8):
                o, free = tile_out(dve, at, k % 2 == 1)
                dve.scalar_tensor_tensor(out=xT[:, k, :], in0=o[:, 0:T], scalar=mod[:, 16 + k, 0:1], in1=xT[:, k, :],
                                         op0=ALU.mult, op1=ALU.add).then_inc(free, 1)
            phase(dve, 5)
            norm_inverse(dve, at, chain, rs2)
            for k in range(KT):
                dve.scalar_tensor_tensor(out=u2T[:, k, :], in0=xT[:, k, :], scalar=A2[:, k:k + 1],
                                         in1=rs2, op0=ALU.mult, op1=ALU.mult).then_inc(sem("u2_scaled"), 1)
            dve.wait_ge(sem("logits"), 1)
            for t in range(TT):
                chain(dve.tensor_tensor(lg[:, t, :], bank[:, 4, t * NE:(t + 1) * NE], prm("router_b", 0, NE), ALU.add))
                chain(dve.max(top[:, t, :], lg[:, t, :]))
                chain(dve.max_index(topi[:, t, :], top[:, t, :], lg[:, t, :]))
                chain(dve.tensor_copy(topf[:, t, :], topi[:, t, :]))
                dve.tensor_scalar(ntop[:, t:t + 1], top[:, t, 0:1], -1.0, None, ALU.mult).then_inc(sem("top_negated"), 1)
                chain(dve.tensor_scalar(chosen[:, t, :], cst("iota"), topf[:, t, 0:1], None, ALU.is_equal))
                for j in range(1, TOPK):
                    ins = dve.scalar_tensor_tensor(out=chosen[:, t, :], in0=cst("iota"), scalar=topf[:, t, j:j + 1],
                                                   in1=chosen[:, t, :], op0=ALU.is_equal, op1=ALU.add)
                    if j < TOPK - 1:
                        chain(ins)
                ins.then_inc(sem("chosen_ready"), 1)
            for c in (0, NE + 1):
                chain(dve.memset(gate[:, :, c:c + 1], 0.0))
            for t in range(TT):
                dve.wait_ge(sem("gate_exps"), t + 1)
                dve.wait_ge(sem("chosen_ready"), t + 1)
                chain(dve.tensor_tensor(gate[:, t, 1:NE + 1], gate[:, t, 1:NE + 1], chosen[:, t, :], ALU.mult))
                chain(dve.reduce_sum(gsum[:, t:t + 1], gate[:, t, 1:NE + 1], AX_X))
                chain(dve.reciprocal(gsum[:, t:t + 1], gsum[:, t:t + 1]))
                dve.tensor_scalar(gate[:, t, 1:NE + 1], gate[:, t, 1:NE + 1], gsum[:, t:t + 1], None, ALU.mult)\
                   .then_inc(sem("gate_ready"), 1)
            dve.wait_ge(sem("gate_ready"), TT)
            chain(dve.memset(place[:, :, :], -1.0))
            dve.wait_ge(sem("ranked"), 1)
            for t in range(TT):
                chain(dve.scalar_tensor_tensor(out=place[:, t, 1:NE + 1], in0=bank[:, 5, t * NE:(t + 1) * NE], scalar=1.0,
                                               in1=chosen[:, t, :], op0=ALU.add, op1=ALU.mult))
                chain(dve.tensor_scalar(place[:, t, 1:NE + 1], place[:, t, 1:NE + 1], -1.0, None, ALU.add))
            chain(dve.reduce_max(gsum[:, 0:1], bank[:, 5, 2 * NE:3 * NE], AX_X))
            dve.tensor_copy(most_i[:, :], gsum[:, 0:1]).then_inc(sem("most_known"), 1)
            chain(dve.tensor_copy(slots[:, :], cst("slot")))

            for b in range(4):
                dve.wait_ge(sem("b2_gated"), b + 1)
                dve.tensor_copy(yacc[:, 2 * b:2 * b + 2, :], bank[:, b, :].rearrange("p (a b) -> p a b", a=2))

            def select(c, n, x):
                for t in range(TT):
                    ins = dve.tensor_scalar(sel[:, t, :], slots[:, :], place[:, t, bass.ds(c, 1)], None, ALU.is_equal)
                ins.then_inc(sem(x + "sel_ready"), 1)

            def select_gates(c, n, x):
                for t in range(TT):
                    ins = dve.tensor_scalar(selg[:, t, :], slots[:, :], place[:, t, bass.ds(c, 1)],
                                            gate[:, t, bass.ds(c, 1)], ALU.is_equal, ALU.mult)
                ins.then_inc(sem(x + "selg_ready"), 1)

            def accumulate(m, x):
                for b, at_bank in enumerate((*GATE_BANKS, LINEAR_BANKS[2])):
                    dve.wait_ge(sem(x + "scattered"), m * 4 + (b + 1))
                    dve.tensor_tensor(yacc[:, 2 * b:2 * b + 2, :], yacc[:, 2 * b:2 * b + 2, :],
                                      bank[:, at_bank, :].rearrange("p (a b) -> p a b", a=2), ALU.add)\
                       .then_inc(sem(x + "acc_read"), 1)

            def expert_dve(i, m, e, used, u0, x):
                lc = LoopChain(dve, sem(x + "expert_chain"), i, 6)
                select_gates(e, m, x)
                dve.wait_ge(sem(x + "xe_ready"), m + 1)
                select(e + 2, m, x)
                dve.wait_ge(sem(x + "w1_round"), i * 2 + 2)
                dve.tensor_copy(ht[:, 1, :], bank[:, 1, :]).then_inc(sem(x + "ht1_ready"), 1)

                def activate(r):
                    dve.wait_ge(sem(x + "sig_ready"), i * 3 + (r + 1))
                    for q, b, g, n in pieces(ROUNDS[r]):
                        ins = dve.tensor_tensor(actT[:, 2 * b:2 * b + 2, g * GROUP:(g + n) * GROUP],
                                                hl[:, r % 2, :, q * GROUP:(q + n) * GROUP],
                                                sgm[:, r % 2, :, q * GROUP:(q + n) * GROUP], ALU.mult)
                    ins.then_inc(sem(x + "act_ready"), 1)

                for r, tasks in enumerate(ROUNDS):
                    if r == 2:
                        dve.wait_ge(sem(x + "act_ready"), i * 3 + 1)
                    dve.wait_ge(sem(x + "h_turned"), i * 3 + (r + 1))
                    h = bank[:, GATE_BANKS[r], :]
                    for q, b, g, n in pieces(tasks):
                        for c in range(2):
                            dst = hg[:, r % 2, c, q * GROUP:(q + n) * GROUP]
                            ins = dve.tensor_scalar(dst, h[:, c * P + q * GROUP:c * P + (q + n) * GROUP],
                                                    par[:, bass.ds(e * 16 + (PARAM["b1"][0] + 4 * b + c), 1)], LIMIT,
                                                    ALU.add, ALU.min)
                    ins.then_inc(sem(x + "biased"), 1)
                    dve.wait_ge(sem(x + "biased"), i * 3 + (r + 1))
                    dve.wait_ge(sem(x + "linear_biased"), i * 3 + (r + 1))
                    lc(dve.tensor_scalar(hl[:, r % 2, :, :], hl[:, r % 2, :, :], LIMIT, -LIMIT, ALU.min, ALU.max))
                    lc(dve.scalar_tensor_tensor(out=hl[:, r % 2, :, :], in0=hl[:, r % 2, :, :], scalar=1.0,
                                                in1=hg[:, r % 2, :, :], op0=ALU.add, op1=ALU.mult))
                    if r >= 1:
                        activate(r - 1)
                activate(2)
                lc.end()
                accumulate(m, x)

            phase(dve, 6)
            select(1, 0, "")
            with dve.Fori(0, NE) as e:
                expert_dve(e, e, e, "unit_used", MOE0, "")
            select_gates(NE, NE, "")
            accumulate(NE, "")
            phase(dve, 7)
            most = dve.value_load(most_i[0:1, 0:1], min_val=0, max_val=T)
            with dve.If(most > SLOTS):
                with dve.Fori(0, PASSES - 1) as b:
                    dve.tensor_scalar(slots[:, :], slots[:, :], float(SLOTS), None, ALU.add).then_inc(sem("more_slots"), 1)
                    dve.wait_ge(sem("more_slots"), b + 1)
                    select(1, 0, "more_")
                    with dve.Fori(0, NE) as e:
                        expert_dve(b * NE + e, b * (NE + 1) + e, e, "more_used", R, "more_")
                    select_gates(NE, NE, "more_")
                    accumulate(b * (NE + 1) + NE, "more_")
            with dve.Else():
                dve.nop()
            phase(dve, 8)
            for k in range(KT):
                ins = dve.scalar_tensor_tensor(out=xT[:, k, :], in0=yacc[:, k, :], scalar=mod[:, 40 + k, 0:1],
                                               in1=xT[:, k, :], op0=ALU.mult, op1=ALU.add)
            ins.then_inc(sem("x2_ready"), 1)
            norm_inverse(dve, at, chain, rs2)
            for k in range(KT):
                dve.scalar_tensor_tensor(out=xT[:, k, :], in0=xT[:, k, :], scalar=prm("final_g", k),
                                         in1=rs2, op0=ALU.mult, op1=ALU.mult)
            phase(dve, 9)
            def pre_norm(g):
                norm_inverse(dve, at, chain, rsb)
                for k in range(KT):
                    dve.scalar_tensor_tensor(out=ub[:, k, :], in0=hT[:, k, :], scalar=prm(g, k), in1=rsb,
                                             op0=ALU.mult, op1=ALU.mult).then_inc(sem("ub_ready"), 1)

            def post_norm(g):
                norm_inverse(dve, at, chain, rsb)
                for k in range(KT):
                    ins = dve.scalar_tensor_tensor(out=ym[:, k, :], in0=ym[:, k, :], scalar=prm(g, k), in1=rsb,
                                                   op0=ALU.mult, op1=ALU.mult)
                chain(ins)
                chain(dve.tensor_tensor(hT[:, :, :], hT[:, :, :], ym[:, :, :], ALU.add))

            def conv(dst, src, w, b, taps, last):
                chain(dve.tensor_scalar(dst, src[:, 0:L], w(0), b, ALU.mult, ALU.add))
                for k in range(1, taps):
                    ins = dve.scalar_tensor_tensor(out=dst, in0=src[:, k:k + L], scalar=w(k), in1=dst,
                                                   op0=ALU.mult, op1=ALU.add)
                    if k < taps - 1 or last is None:
                        chain(ins)
                    else:
                        ins.then_inc(last, 1)

            def ffn(n):
                pre_norm(f"f{n}_pre")

                def gated(j):
                    dve.wait_ge(sem("ffn_gelu"), at.ffn + j + 1)
                    dve.tensor_tensor(actF[:, j, :], gl[:, j % 2, :], cv[:, j % 2, 1, :], ALU.mult)\
                       .then_inc(sem("ffn_act"), 1)

                chain(dve.memset(up[:, :, :, 0:2], 0.0))
                for j in range(FT):
                    for c in range(2):
                        o, free = tile_out(dve, at, c == 1)
                        dve.wait_ge(free, (at.out + 1) // NL)
                        i = 2 * j + c
                        conv(cv[:, j % 2, c, :], up[:, j % 2, c, :], lambda k: prm(f"f{n}_cw", k * 44 + i),
                             prm(f"f{n}_cb", i), 3, sem("ffn_conv") if c == 1 else None)
                    if j >= 1:
                        gated(j - 1)
                gated(FT - 1)
                at.ffn += FT

            at.ffn = 0
            at.unit = TAIL0
            pre_norm("l0_pre")
            chain(dve.memset(xr[:, :, 0:3], 0.0))
            dve.wait_ge(sem("lam_exps"), 1)
            log1p(dve, chain, lru1[:, :], lru3[:, :], nlru[:, :])
            chain(dve.tensor_scalar(lru2[:, :], prm("lru_lam", 0, 8), -1.0, 0.0, ALU.mult, ALU.max))
            chain(dve.tensor_tensor(lru2[:, :], lru2[:, :], lru1[:, :], ALU.add))
            chain(dve.tensor_scalar(lru2[:, :], lru2[:, :], LRU_C, None, ALU.mult))
            dve.tensor_scalar(nlru[:, :], lru2[:, :], -1.0, None, ALU.mult).then_inc(sem("nlru_ready"), 1)
            for n in range(8):
                tile_skip(at, n % 2 == 1)
            for n in range(8):
                o, free = tile_out(dve, at, n % 2 == 1)
                dve.wait_ge(free, (at.out + 1) // NL)
                conv(xc[:, n, :], xr[:, n, :], lambda k: prm("lru_cw", k * 8 + n), prm("lru_cb", n), 4, sem("xc_ready"))
            for n in range(10):
                tile_skip(at, n % 2 == 1)
            dve.wait_ge(sem("lru_decay"), 8)
            dve.wait_ge(sem("xc_ready"), 8)
            chain(dve.memset(smx[:, :, :], 0.0))
            chain(dve.memset(sden[:, :, :], 1.0))
            phase(dve, 10)

            def swa_scores(i):
                b = i % 2
                dve.wait_ge(sem("swa_scores"), i + 1)
                for part, (a, w, n) in enumerate(((0, 3 * P, P), (3 * P, L, META))):
                    ins = dve.scalar_tensor_tensor(out=sc[0:n, i % 3, a:a + w], in0=cst("pen", a, w)[0:n, :],
                                                   scalar=cst("slope", i, 1)[0:n, :],
                                                   in1=bank[0:n, 2 * (i % 3) + part, 0:w], op0=ALU.mult, op1=ALU.add)
                chain(ins)
                for t, (t0, n) in enumerate(TOK):
                    ins = dve.reduce_max(smx[0:n, b, t:t + 1], sc[0:n, i % 3, SC[t]:SC[t] + t0 + n], AX_X)
                chain(ins)
                chain(dve.tensor_scalar(smx[:, b, :], smx[:, b, :], HD ** -0.5, prm("sinks", i), ALU.mult, ALU.max))
                dve.tensor_scalar(snm[:, b, :], smx[:, b, :], -1.0, None, ALU.mult).then_inc(sem("swa_negmax"), 1)

            def swa_probs(i):
                b = i % 2
                dve.wait_ge(sem("swa_exp"), i + 1)
                chain(dve.tensor_tensor(ssk[:, b, :], ssk[:, b, :], sden[:, b, :], ALU.add))
                chain(dve.reciprocal(ssk[:, b, :], ssk[:, b, :]))
                for t, (t0, n) in enumerate(TOK):
                    s = sc[0:n, i % 3, SC[t]:SC[t] + t0 + n]
                    ins = dve.tensor_scalar(s, s, ssk[0:n, b, t:t + 1], None, ALU.mult)
                ins.then_inc(sem("swa_probs"), 1)

            def lru_input(n):
                chain(dve.tensor_scalar(mix[:, n, :], th[:, n, :], 1.0, None, ALU.add))
                chain(dve.reciprocal(mix[:, n, :], mix[:, n, :]))
                dve.tensor_tensor(th[:, n, :], th[:, n, :], mix[:, n, :], ALU.mult).then_inc(sem("lru_ratio"), 1)
                chain(dve.tensor_tensor(xc[:, n, :], xc[:, n, :], ig[:, n, :], ALU.mult))

            def lru_scan(n):
                dve.wait_ge(sem("lru_root"), 1)
                chain(dve.tensor_tensor(xc[:, n, :], xc[:, n, :], th[:, n, :], ALU.mult))
                chain(dve.tensor_tensor_scan(out=ig[:, n, :], data0=rg[:, n, :], data1=xc[:, n, :], initial=0.0,
                                             op0=ALU.mult, op1=ALU.add))
                chain(dve.tensor_tensor(mix[:, n, :], ga[:, n, :], ig[:, n, :], ALU.mult))

            swa_scores(0)
            for i in range(HEADS2):
                if i < HEADS2 - 1:
                    if i >= 2:
                        dve.wait_ge(sem("swa_turned"), i - 1)
                    swa_scores(i + 1)
                swa_probs(i)
                if i < 8:
                    lru_input(i)
                else:
                    lru_scan(i - 8)
            phase(dve, 11)
            for k in range(KT):
                tile_skip(at, True)
            post_norm("l0_post")
            phase(dve, 12)
            ffn(0)
            at.unit += 2 * KT
            at.out += KT
            post_norm("f0_post")
            phase(dve, 13)
            chain(dve.memset(xp[:, :, 0:3], 0.0))
            phase(dve, 14)
            pre_norm("l1_pre")
            for n in range(ST):
                tile_skip(at, n % 2 == 1)
            for n in range(CT):
                o, free = tile_out(dve, at, n % 2 == 1)
                dve.wait_ge(free, (at.out + 1) // NL)
                if n >= 4:
                    dve.wait_ge(sem("ssm_silu"), n - 3)
                conv(xv[:, n % 4, :], xp[:, n % 4, :], lambda k: prm("ssm_cw", k * CT + n), prm("ssm_cb", n), 4,
                     sem("ssm_conv"))
            dve.wait_ge(sem("dt_step"), 1)
            dve.tensor_scalar(dtr[0:SH, :], bank[0:SH, 4, 0:L], prm("dt_bias")[0:SH, :], None, ALU.add)\
               .then_inc(sem("dt_step"), 1)
            dve.wait_ge(sem("dt_step"), 3)
            log1p(dve, chain, dt1[0:SH, :], dt2[0:SH, :], dt3[0:SH, :])
            chain(dve.scalar_tensor_tensor(out=dtr[0:SH, :], in0=dtr[0:SH, :], scalar=0.0, in1=dt1[0:SH, :],
                                           op0=ALU.max, op1=ALU.add))
            chain(dve.tensor_scalar(dt1[0:SH, :], dtr[0:SH, :], acl[0:SH, 0:1], -1.0, ALU.mult, ALU.mult))
            chain(dve.memset(dt2[0:SH, :], 0.0))
            chain(dve.tensor_tensor_scan(out=csr[0:SH, :], data0=dt1[0:SH, :], data1=dt2[0:SH, :], initial=0.0,
                                         op0=ALU.add, op1=ALU.add))
            phase(dve, 15)
            phase(dve, 16)

            def ssm_args(h):
                if h % 4 == 0:
                    g = h // 4
                    dve.wait_ge(sem("ssm_cb"), g + 1)
                    m = cst("causal")
                    dve.tensor_tensor(cbm[:, g % 2, 0:SEG[2]], bank[:, g % 2, 0:SEG[2]], m[:, 0:SEG[2]], ALU.mult)
                    dve.tensor_tensor(cbm[0:META, g % 2, SEG[2]:], bank[0:META, g % 2, SEG[2]:STRIP],
                                      m[0:META, SEG[2]:STRIP], ALU.mult).then_inc(sem("cb_read"), 1)
                dve.wait_ge(sem("ssm_rows"), h + 1)
                if h >= 2:
                    dve.wait_ge(sem("ssm_weights"), h - 1)
                for c, (t0, n) in enumerate(TOK):
                    ins = dve.tensor_scalar(dec[0:n, h % 2, SEG[c]:SEG[c] + L - t0],
                                            bank[0:n, ROW_BANKS[h % 3], SEG[c]:SEG[c] + L - t0],
                                            csc[0:n, c, h:h + 1], 0.0, ALU.add, ALU.min)
                ins.then_inc(sem("ssm_args"), 1)

            def ssm_weights(h):
                dve.wait_ge(sem("ssm_decay"), h + 1)
                dve.wait_ge(sem("cb_read"), h // 4 + 1)
                if h >= 2:
                    dve.wait_ge(sem("ssm_y"), h - 1)
                for c, (t0, n) in enumerate(TOK):
                    seg = slice(SEG[c], SEG[c] + L - t0)
                    ins = dve.scalar_tensor_tensor(out=wts[0:n, h % 2, seg], in0=dec[0:n, h % 2, seg],
                                                   scalar=dtc[0:n, c, h:h + 1], in1=cbm[0:n, (h // 4) % 2, seg],
                                                   op0=ALU.mult, op1=ALU.mult)
                ins.then_inc(sem("ssm_weights"), 1)

            def ssm_result(n):
                dve.wait_ge(sem("ssm_y"), 2 * n + 2)
                dve.scalar_tensor_tensor(out=xb[:, n, :], in0=xb[:, n, :], scalar=prm("d_skip", n),
                                         in1=bank[:, 4 + n % 2, 0:L], op0=ALU.mult, op1=ALU.add)\
                   .then_inc(sem("ssm_y_read"), 1)
                dve.wait_ge(sem("ssm_y_read"), n + 1)
                chain(dve.tensor_tensor(zs[:, n, :], zs[:, n, :], xb[:, n, :], ALU.mult))

            ssm_args(0)
            for h in range(SH):
                if h < SH - 1:
                    ssm_args(h + 1)
                ssm_weights(h)
                if h % 2 == 0 and h >= 2:
                    ssm_result(h // 2 - 1)
            ssm_result(SH // 2 - 1)
            phase(dve, 17)
            for g in range(SG):
                dve.wait_ge(sem("group_root"), g + 1)
                chain(dve.reciprocal(rs16[:, g, :], rs16[:, g, :]))
                for n in (2 * g, 2 * g + 1):
                    chain(dve.scalar_tensor_tensor(out=zs[:, n, :], in0=zs[:, n, :], scalar=prm("gnorm", n),
                                                   in1=rs16[:, g, :], op0=ALU.mult, op1=ALU.mult))
            phase(dve, 18)
            for k in range(KT):
                tile_skip(at, True)
            post_norm("l1_post")
            phase(dve, 19)
            ffn(1)
            at.unit += 2 * KT
            at.out += KT
            post_norm("f1_post")
            phase(dve, 20)

        @block.gpsimd
        def _(pool):
            for n in range(1, 6):
                phase(pool, n)
            pool.memset(ys[:, :], 0.0).then_inc(sem("ys_ready"), 1)
            pool.dma_start(b2r[0:NE, :], dram["b2rows"]).then_inc(sem("b2_loaded"), 16)
            for n in range(6, LAST_PHASE + 1):
                phase(pool, n)

        @block.tensor
        def _(pe):
            at = Count()
            def ada_unit(k, b):
                s = slot_filled(pe, at)
                for q in range(4):
                    mm = pe.matmul(bank[q * 32:(q + 1) * 32, b, :],
                                   cact[:, 2 * k:2 * k + 2, :],
                                   ring[:, s, q * 512:(q + 1) * 512], start=(k == 0), stop=(k == KT - 1))
                mm.then_inc(sem("unit_used"), 1)
                at.unit += 1

            def ada_turn(j, b):
                for c in range(4):
                    mm = pe.transpose(bank[:, b, c * P:(c + 1) * P], ada[:, j, c * P:(c + 1) * P], ident)
                mm.then_inc(sem("ada_turned"), 1)

            pe.wait_ge(sem("c_ready"), 1)
            for k in range(R):
                ada_unit(k, 6)
            pe.wait_ge(sem("con_loaded"), 80)
            norm_sums(pe, at, lambda k: sq.rearrange("p a (b c) -> p (a b) c", c=512)[:, k, :], 512)
            for k in range(R, KT):
                ada_unit(k, 6)
            pe.wait_ge(sem("ada_copied"), 1)
            ada_turn(0, 7)

            def u_lat(k):
                return u[:, k, lat]

            def u_all(k):
                return u[:, k, :]

            def u_tok(k, t):
                return u[:, k, t * P:(t + 1) * P]

            pe.wait_ge(sem("u_ready"), KT)
            for t in range(4):
                for k in range(KT):
                    mm = pe.matmul(bank[:, 4, t * 16:(t + 1) * 16], u_tok(k, t), wg[:, k, :],
                                   start=(k == 0), stop=(k == KT - 1))
            mm.then_inc(sem("gates_done"), 1)
            project(pe, at, 2, u_lat, T)
            project(pe, at, 2, u_all, 2 * T)
            project_tokens(pe, at, 4, u_tok, 4)
            pe.wait_ge(sem("logf_ready"), 1)
            for d in range(2):
                for kind in range(2):
                    for t in range(4):
                        c = 8 * d + 4 * kind
                        mm = pe.transpose(bank[0:4, 2 * d + kind, t * P:(t + 1) * P], gtok[:, t, c:c + 4], ident)
            mm.then_inc(sem("gates_turned"), 1)
            project(pe, at, 4, u_lat, T)
            project(pe, at, 4, u_lat, T)
            pe.wait_ge(sem("rows_ready"), 1)
            for d in range(2):
                for c in range(4):
                    mm = pe.transpose(bank[:, 4, (4 * d + c) * 4:(4 * d + c) * 4 + 4],
                                      arow[0:4, d, c * P:(c + 1) * P], cst("ident")[0:4, 0:4])
            mm.then_inc(sem("acol_turned"), 1)
            project(pe, at, 4, u_all, 2 * T)
            project_tokens(pe, at, 4, u_tok, 4)
            pe.wait_ge(sem("bank_read0"), at.out // 2)
            pe.wait_ge(sem("bank_read1"), at.out // 2)

            def m_scores(h):
                for c in range(4):
                    pe.matmul(bank[:, c // 2, (c % 2) * T:(c % 2 + 1) * T], km[:, h, c * P:(c + 1) * P], qm[:, h, :],
                              start=True, stop=True)

            def m_rows(i):
                h, d = i // 2, i % 2
                if i >= 2:
                    pe.wait_ge(sem("decay_ready"), i - 1)
                pe.matmul(bank[:, 2 + i % 2, :], cst("ident", h, 1)[0:4, :].to_broadcast([4, P]), crow[0:4, d, :, :],
                          start=True, stop=True).then_inc(sem("m_rows"), 1)

            m_scores(0)
            m_rows(0)
            for i in range(8):
                h = i // 2
                if i < 7:
                    m_rows(i + 1)
                for n in (2 * i, 2 * i + 1):
                    ada_unit(n % KT, 6 + n // KT)
                pe.wait_ge(sem("m_weights"), i + 1)
                if i % 2 == 1 and h < 3:
                    m_scores(h + 1)
                if i >= 1:
                    pe.wait_ge(sem("m_fin"), i)
                for j in range(2):
                    for c in range(4):
                        pe.matmul(bank[:, 4, j * T:(j + 1) * T], vm[:, c, h * DV_M + j * P:h * DV_M + (j + 1) * P],
                                  PM[:, i % 2, c, :], start=(c == 0), stop=(c == 3))
                for c in range(4):
                    mm = pe.matmul(bank[:, 5, 0:T], ones, PM[:, i % 2, c, :], start=(c == 0), stop=(c == 3))
                mm.then_inc(sem("m_sums"), 1)
            pe.wait_ge(sem("decay_ready"), 8)
            for n in range(2 * NH_D):
                x = qd[:, n, :] if n < NH_D else kd[:, n - NH_D, lat]
                if n >= 2:
                    pe.wait_ge(sem("rot_read"), n - 1)
                pe.matmul(bank[:, 2 + n % 2, 0:T], cst("perm"), x, start=True, stop=True).then_inc(sem("rotated"), 1)
            phase(pe, 1)
            for k in range(KT):
                pe.wait_ge(sem("squares"), at.norm + k + 1)
                h = k // 2
                mm = pe.matmul(bank[:, h // 2, (h % 2) * T:(h % 2 + 1) * T], ones, sq8[:, k, :],
                               start=(k % 2 == 0), stop=(k % 2 == 1))
            at.norm += KT
            mm.then_inc(sem("head_sums"), 1)
            pe.wait_ge(sem("ada_copied"), 2)
            for j in range(2):
                ada_turn(j, 2 + j)
            phase(pe, 2)
            pe.wait_ge(sem("lambda_step"), 1)
            pe.matmul(bank[:, 4, 0:2], ones, lamc[:, 0:2], start=True, stop=True).then_inc(sem("lambda_step"), 1)
            pe.wait_ge(sem("lambda_step"), 3)

            def d_scores(h):
                for j in range(4):
                    m, qt = j // 2, j % 2
                    if h >= 1:
                        pe.wait_ge(sem("probs"), 4 * h + j - 3)
                    pe.matmul(bank[:, j, :], qd[64 * m:64 * m + 64, h, qt * P:(qt + 1) * P],
                              kd[64 * m:64 * m + 64, h, :], start=True, stop=True).then_inc(sem("scores"), 1)

            d_scores(0)
            for h in range(NH_D):
                if h < NH_D - 1:
                    d_scores(h + 1)
                for qt in range(2):
                    pe.wait_ge(sem("a_ready"), 2 * h + qt + 1)
                    if h >= 1:
                        pe.wait_ge(sem("aT_ready"), 2 * h + qt - 1)
                    for c in range(4):
                        mm = pe.transpose(bank[:, 4 + qt, c * P:(c + 1) * P], PA[:, h % 2, qt, c * P:(c + 1) * P], ident)
                    mm.then_inc(sem("a_turned"), 1)
                pe.wait_ge(sem("aT_ready"), 2 * h + 2)
                if h >= 2:
                    pe.wait_ge(sem("bout_ready"), h - 1)
                for c in range(4):
                    mm = pe.matmul(bank[:, 6 + h % 2, 0:T], vd[:, c, h * P:(h + 1) * P], aT[:, c, :],
                                   start=(c == 0), stop=(c == 3))
                mm.then_inc(sem("d_out"), 1)
            phase(pe, 3)
            for k in range(KT):
                pe.wait_ge(sem("squares"), at.norm + k + 1)
                mm = pe.matmul(bank[:, k // 2, (k % 2) * T:(k % 2 + 1) * T], ones, sq8[:, k, :], start=True, stop=True)
            at.norm += KT
            mm.then_inc(sem("head_sums"), 1)
            phase(pe, 4)
            for p in range(4):
                project(pe, at, 1, u_lat, T)
                project(pe, at, 1, lambda k: aout[:, k, :], T)
                project(pe, at, 1, u_lat, T)
                project(pe, at, 1, lambda k: bout[:, k, :], T)
            pe.wait_ge(sem("merged"), 1)
            project(pe, at, 4, lambda k: y1[:, k, :], T)
            phase(pe, 5)
            norm_sums(pe, at, lambda k: sq2[:, k, :], T)
            pe.wait_ge(sem("u2_ready"), KT)
            for t in range(TT):
                for b in range(2):
                    for c in range(4):
                        mm = pe.transpose(bank[:, 2 * t + b, c * P:(c + 1) * P],
                                          u2T[:, 4 * b + c, t * P:(t + 1) * P], ident)
                    mm.then_inc(sem("u2_turned"), 1)
            for t in range(TT):
                for k in range(KT):
                    mm = pe.matmul(bank[:, 4, t * NE:(t + 1) * NE], u2T[:, k, t * P:(t + 1) * P], wr[:, k, :],
                                   start=(k == 0), stop=(k == KT - 1))
            mm.then_inc(sem("logits"), 1)
            pe.wait_ge(sem("chosen_ready"), 2)
            pe.wait_ge(sem("norm_root"), 2)
            pe.matmul(bank[:, 5, 0:NE], cst("before"), chosen[:, 0, :], start=True, stop=True)
            pe.matmul(bank[:, 5, NE:2 * NE], cst("before"), chosen[:, 1, :], start=True, stop=False)
            pe.matmul(bank[:, 5, NE:2 * NE], ones, chosen[:, 0, :], start=False, stop=True)
            pe.matmul(bank[:, 5, 2 * NE:3 * NE], ones, chosen[:, 0, :], start=True, stop=False)
            pe.matmul(bank[:, 5, 2 * NE:3 * NE], ones, chosen[:, 1, :], start=False, stop=True)\
              .then_inc(sem("ranked"), 1)
            pe.wait_ge(sem("gate_ready"), TT)
            for t in range(TT):
                mm = pe.transpose(bank[0:NE, 6, t * P:(t + 1) * P], gate[:, t, 1:NE + 1], ident)
            mm.then_inc(sem("gate_turned"), 1)
            pe.wait_ge(sem("gateT_ready"), 1)
            pe.wait_ge(sem("b2_loaded"), 16)
            for o in range(KT):
                mm = pe.matmul(bank[:, o // 2, (o % 2) * T:(o % 2 + 1) * T], b2r[0:NE, o * P:(o + 1) * P], gateT[0:NE, :],
                               start=True, stop=True)
                if o % 2 == 1:
                    mm.then_inc(sem("b2_gated"), 1)
            phase(pe, 6)

            def gather(n, x):
                pe.wait_ge(sem(x + "sel_ready"), n)
                for k in range(KT):
                    for t in range(TT):
                        mm = pe.matmul(bank[:, 4 + k // 4, (k % 4) * SLOTS:(k % 4 + 1) * SLOTS],
                                       u2tok[:, t, k * P:(k + 1) * P], sel[:, t, :], start=(t == 0), stop=(t == TT - 1))
                mm.then_inc(sem(x + "gathered"), 1)

            def turn_gates(n, x):
                pe.wait_ge(sem(x + "selg_ready"), n)
                for t in range(TT):
                    mm = pe.transpose(bank[0:SLOTS, 4, t * P:(t + 1) * P], selg[:, t, :], ident)
                mm.then_inc(sem(x + "sg_turned"), 1)

            def scatter(blocks, n_ys, n_sg, x, rounds=None):
                pe.wait_ge(sem(x + "ys_ready"), n_ys)
                pe.wait_ge(sem(x + "sgT_ready"), n_sg)
                for b in blocks:
                    at_bank = (*GATE_BANKS, LINEAR_BANKS[2])[b]
                    if rounds is not None:
                        if b < 3:
                            pe.wait_ge(sem(x + "biased"), rounds + (b + 1))
                        else:
                            pe.wait_ge(sem(x + "linear_biased"), rounds + 3)
                    for c in range(2):
                        o = 2 * b + c
                        mm = pe.matmul(bank[:, at_bank, c * T:(c + 1) * T], ys[0:SLOTS, o * P:(o + 1) * P],
                                       sgT[0:SLOTS, :, :], start=True, stop=True)
                    mm.then_inc(sem(x + "scattered"), 1)

            def expert_pe(i, m, filled, used, u0, x):

                def unit(j):
                    n = u0 + j
                    s = n % R
                    pe.wait_ge(sem(f"{filled}{s}"), i * (16 * (EU // R)) + 16 * (n // R + 1))
                    return s

                pe.wait_ge(sem(x + "xe_ready"), m + 1)
                turn_gates(m + 1, x)
                for k in range(KT):
                    s = unit(k)
                    for r, tasks in enumerate(ROUNDS):
                        for q, (b, g) in enumerate(tasks):
                            mm = pe.matmul(bank[q * GROUP:(q + 1) * GROUP, r, :], xe[:, k, g * GROUP:(g + 1) * GROUP],
                                           ring[:, s, b * 512:(b + 1) * 512], start=(k == 0), stop=(k == KT - 1))
                        if k == KT - 1 and r < 2:
                            mm.then_inc(sem(x + "w1_round"), 1)
                    mm.then_inc(sem(used), 1)
                pe.wait_ge(sem(x + "sgT_ready"), m + 1)
                for r in range(3):
                    if r == 1:
                        pe.wait_ge(sem(x + "ht1_ready"), i + 1)
                    else:
                        pe.wait_ge(sem(x + "ht_ready"), i * 2 + (r // 2 + 1))
                    for c in range(4):
                        mm = pe.transpose(bank[:, (GATE_BANKS, LINEAR_BANKS)[c // 2][r], (c % 2) * P:(c % 2 + 1) * P], ht[:, r, c * P:(c + 1) * P], ident)
                    mm.then_inc(sem(x + "h_turned"), 1)
                scatter((0,), i + 1, m + 1, x, i * 3)
                pe.wait_ge(sem(x + "linear_biased"), i * 3 + 2)
                gather(m + 2, x)
                scatter((1, 2, 3), i + 1, m + 1, x, i * 3)
                pe.wait_ge(sem(x + "act_ready"), i * 3 + 3)
                for j in range(4):
                    s = unit(KT + j)
                    for c in range(2):
                        k = 2 * j + c
                        for r, tasks in enumerate(ROUNDS):
                            for q, (b, g) in enumerate(tasks):
                                mm = pe.matmul(bank[q * GROUP:(q + 1) * GROUP, 6 + r // 2, (r % 2) * 256:(r % 2 + 1) * 256],
                                               actT[:, k, g * GROUP:(g + 1) * GROUP],
                                               ring[:, s, c * D + b * 256:c * D + (b + 1) * 256],
                                               start=(k == 0 and r != 1), stop=(k == KT - 1), skip_group_check=True)
                    mm.then_inc(sem(used), 1)
                pe.wait_ge(sem(x + "acc_read"), m * 4 + 4)

            gather(1, "")
            with pe.Fori(0, NE) as e:
                expert_pe(e, e, "filled", "unit_used", MOE0, "")
            pe.wait_ge(sem("xe_ready"), NE + 1)
            turn_gates(NE + 1, "")
            scatter(range(4), NE + 1, NE + 1, "")
            phase(pe, 7)
            most = pe.value_load(most_i[0:1, 0:1], min_val=0, max_val=T)
            with pe.If(most > SLOTS):
                with pe.Fori(0, PASSES - 1) as b:
                    m0 = b * (NE + 1)
                    gather(m0 + 1, "more_")
                    with pe.Fori(0, NE) as e:
                        expert_pe(b * NE + e, m0 + e, "more_filled", "more_used", 0, "more_")
                    pe.wait_ge(sem("more_xe_ready"), m0 + (NE + 1))
                    turn_gates(m0 + (NE + 1), "more_")
                    scatter(range(4), b * NE + (NE + 1), m0 + (NE + 1), "more_")
                    pe.wait_ge(sem("more_acc_read"), m0 * 4 + 4 * (NE + 1))
            with pe.Else():
                pe.nop()
            phase(pe, 8)
            at.unit = TAIL0
            norm_sums(pe, at, lambda k: sq2[:, k, :], T)
            phase(pe, 9)
            def ub_k(k):
                return ub[:, k, :]

            def pre_norm():
                norm_sums(pe, at, lambda k: sqb[:, k, :], L)
                at.ub += KT
                pe.wait_ge(sem("ub_ready"), at.ub)

            def post_norm():
                norm_sums(pe, at, lambda k: sqb[:, k, :], L)

            def ffn():
                pre_norm()
                project(pe, at, FT, ub_k, L)
                at.ffn += FT
                pe.wait_ge(sem("ffn_act"), at.ffn)
                project_deep(pe, at, 2, FT // 2, lambda k: actF[:, k, :], L)
                post_norm()

            at.ub = at.ffn = 0
            pre_norm()
            project(pe, at, 12, ub_k, L)
            s = slot_filled(pe, at)
            o = out_bank(pe, at)
            for k in range(KT):
                mm = pe.matmul(o[:, 0:L], ring[:, s, k * 256:k * 256 + P], ub[:, k, :], start=(k == 0), stop=(k == KT - 1))
            mm.then_inc(sem("tile_done"), 1)
            o = out_bank(pe, at)
            for t, (t0, n) in enumerate(TOK):
                for k in range(KT):
                    mm = pe.matmul(o[0:n, t * P:(t + 1) * P], ub[:, k, t0:t0 + n], ring[:, s, k * 256 + P:(k + 1) * 256],
                                   start=(k == 0), stop=(k == KT - 1))
            mm.then_inc(sem("unit_used"), 1)
            at.unit += 1
            pe.wait_ge(sem("lru_loaded"), 16)
            for n in range(8):
                pe.wait_ge(sem("xc_ready"), n + 1)
                if n >= 2:
                    pe.wait_ge(sem("lru_gate_read"), n - 1)
                b = 2 * (n % 2)
                pe.matmul(bank[:, b, 0:L], wlru[:, 0, n, :], xc[:, n, :], start=True, stop=True)
                pe.matmul(bank[:, b + 1, 0:L], wlru[:, 1, n, :], xc[:, n, :], start=True, stop=True)\
                  .then_inc(sem("lru_gates"), 1)
            phase(pe, 10)

            def swa_scores(i):
                j, s = i // 2, 64 * (i % 2)
                if i >= 3:
                    pe.wait_ge(sem("swa_negmax"), i - 2)
                for t, (t0, n) in enumerate(TOK):
                    o = SC[t] % (3 * P)
                    mm = pe.matmul(bank[0:n, 2 * (i % 3) + t // 2, o:o + t0 + n], q0[s:s + 64, j, t0:t0 + n], k0[s:s + 64, 0:t0 + n],
                                   start=True, stop=True)
                mm.then_inc(sem("swa_scores"), 1)

            def swa_values(i):
                j, s = i // 2, 64 * (i % 2)
                pe.wait_ge(sem("pt_ready"), i + 1)
                if i % 2 == 0 and i >= 2:
                    pe.wait_ge(sem("swa_result"), i // 2)
                for c, (t0, n) in enumerate(TOK):
                    mm = pe.matmul(bank[s:s + 64, 7, t0:L], v0[0:n, c, s:s + 64], pt[0:n, i % 2, SEG[c]:SEG[c] + L - t0],
                                   start=(c == 0), stop=(c == 2), skip_group_check=True)
                mm.then_inc(sem("swa_pv"), 1)

            swa_scores(0)
            swa_scores(1)
            for i in range(HEADS2):
                if i < HEADS2 - 2:
                    swa_scores(i + 2)
                pe.wait_ge(sem("swa_probs"), i + 1)
                if i >= 1:
                    pe.wait_ge(sem("pt_ready"), i)
                for c, (s0, m) in enumerate(TOK):
                    for t in range(c, 3):
                        t0, n = TOK[t]
                        at0 = SEG[c] + t0 - s0
                        mm = pe.transpose(bank[0:m, 6, at0:at0 + n], sc[0:n, i % 3, SC[t] + s0:SC[t] + s0 + m], ident[0:n, 0:n])
                mm.then_inc(sem("swa_turned"), 1)
                if i >= 1:
                    swa_values(i - 1)
            swa_values(HEADS2 - 1)
            phase(pe, 11)
            project_deep(pe, at, 1, 2 * KT, lambda k: mix[:, k, :], L)
            post_norm()
            phase(pe, 12)
            ffn()
            phase(pe, 13)
            phase(pe, 14)
            pre_norm()
            project(pe, at, 24, ub_k, L)
            for k in range(KT):
                mm = pe.matmul(bank[0:SH, 4, 0:L], wdt[:, k, :], ub[:, k, :], start=(k == 0), stop=(k == KT - 1))
            mm.then_inc(sem("dt_step"), 1)
            phase(pe, 15)
            for b in range(12):
                t0, n = TOK[b // 4]
                if b >= 2:
                    pe.wait_ge(sem("x_turn_read"), b - 1)
                for c in range(4):
                    mm = pe.transpose(bank[0:n, b % 2, c * P:(c + 1) * P], xb[:, 4 * (b % 4) + c, t0:t0 + n], ident)
                mm.then_inc(sem("x_turned"), 1)
            for c, (t0, n) in enumerate(TOK):
                pe.transpose(bank[0:n, 2, c * 64:c * 64 + SH], csr[0:SH, t0:t0 + n], ident[0:SH, 0:SH])
                mm = pe.transpose(bank[0:n, 2, c * 64 + SH:c * 64 + 2 * SH], dtr[0:SH, t0:t0 + n], ident[0:SH, 0:SH])
            mm.then_inc(sem("dt_turned"), 1)
            phase(pe, 16)

            def ssm_rows(h):
                if h % 4 == 0:
                    g = h // 4
                    if g >= 2:
                        pe.wait_ge(sem("cb_read"), g - 1)
                    for c, (t0, n) in enumerate(TOK):
                        mm = pe.matmul(bank[0:n, g % 2, SEG[c]:SEG[c] + L - t0], xb[:, ST + g, t0:t0 + n],
                                       xb[:, ST + SG + g, t0:L], start=True, stop=True)
                    mm.then_inc(sem("ssm_cb"), 1)
                if h >= 3:
                    pe.wait_ge(sem("ssm_args"), h - 2)
                for c, (t0, n) in enumerate(TOK):
                    mm = pe.matmul(bank[0:P, ROW_BANKS[h % 3], SEG[c]:SEG[c] + L - t0],
                                   cst("ident", h, 1)[0:SH, :].to_broadcast([SH, P]), csr[0:SH, t0:L],
                                   start=True, stop=True)
                mm.then_inc(sem("ssm_rows"), 1)

            ssm_rows(0)
            ssm_rows(1)
            for h in range(SH):
                if h < SH - 2:
                    ssm_rows(h + 2)
                pe.wait_ge(sem("ssm_weights"), h + 1)
                n, s = h // 2, 64 * (h % 2)
                if n >= 2 and h % 2 == 0:
                    pe.wait_ge(sem("ssm_y_read"), n - 1)
                for c, (t0, m) in enumerate(TOK):
                    mm = pe.matmul(bank[s:s + 64, 4 + n % 2, t0:L], xt[0:m, c, h * HD:(h + 1) * HD],
                                   wts[0:m, h % 2, SEG[c]:SEG[c] + L - t0], start=(c == 0), stop=(c == 2),
                                   skip_group_check=True)
                mm.then_inc(sem("ssm_y"), 1)
            phase(pe, 17)
            for g in range(SG):
                for n in (2 * g, 2 * g + 1):
                    pe.wait_ge(sem("squares"), at.norm + n + 1)
                    mm = pe.matmul(bank[:, g, 0:L], ones, sq16[:, n, :], start=(n % 2 == 0), stop=(n % 2 == 1))
                mm.then_inc(sem("group_sums"), 1)
            at.norm += ST
            phase(pe, 18)
            project_deep(pe, at, 1, ST, lambda k: zs[:, k, :], L)
            post_norm()
            phase(pe, 19)
            ffn()
            phase(pe, 20)



def log1p(dve, chain, e, s, q):
    chain(dve.tensor_scalar(s, e, 2.0, None, ALU.add))
    chain(dve.reciprocal(s, s))
    chain(dve.tensor_tensor(s, s, e, ALU.mult))
    chain(dve.tensor_tensor(e, s, s, ALU.mult))
    chain(dve.tensor_scalar(q, e, 1.0 / 17, None, ALU.mult))
    for n in (15, 13, 11, 9, 7, 5, 3):
        chain(dve.scalar_tensor_tensor(out=q, in0=q, scalar=1.0 / n, in1=e, op0=ALU.add, op1=ALU.mult))
    chain(dve.scalar_tensor_tensor(out=q, in0=q, scalar=1.0, in1=s, op0=ALU.add, op1=ALU.mult))
    chain(dve.tensor_scalar(e, q, 2.0, None, ALU.mult))



def kernel(**inputs):
    import concourse.bacc as bacc
    from concourse.bass_utils import run_bass_kernel_spmd

    arrays = lay_out({name: np.asarray(a) for name, a in inputs.items()})
    nc = bacc.Bacc("TRN2", target_bir_lowering=False, num_devices=1)
    dram = {name: nc.dram_tensor(f"in_{name}", a.shape, F32, kind="ExternalInput").ap()
            for name, a in arrays.items()}
    out = nc.dram_tensor("out", (P, KT, T), F32, kind="ExternalOutput").ap()
    program(nc, dram, out)
    ran = run_bass_kernel_spmd(nc, [{f"in_{name}": a for name, a in arrays.items()}], core_ids=[0])
    got = ran.results[0]["out"]
    return np.ascontiguousarray(got.transpose(2, 1, 0).reshape(1, T, D))
```
